# Optimizing a Trainium2 kernel written in Bass

```python
import math
import jax, jax.numpy as jnp
from jax import lax
import numpy as np

D_MODEL = 1024
BATCH = 1
SEQ = 256
DEPTH = 2
DEC_BATCH = 8
DEC_SEQ = 1
PAST_LEN = 256
PAGE_SIZE = 128

F32 = jnp.float32
EPS = 1e-6

POOL_WIDTH = D_MODEL // 4
POOL_GROUPS = 4
POOL_GROUP_WIDTH = POOL_WIDTH // POOL_GROUPS
POOL_WINDOWS = (2, 4, 8, 16)
POOL_PREV = max(POOL_WINDOWS) - 1

DIFF_HEADS = 4
DIFF_HEAD_DIM = D_MODEL // 16
DIFF_V_DIM = 2 * DIFF_HEAD_DIM
QK_WIDTH = DIFF_HEADS * 2 * DIFF_HEAD_DIM
ATTN_WIDTH = DIFF_HEADS * DIFF_V_DIM
Q_BLOCK = 128

SSM_WIDTH = D_MODEL // 4
SSM_GROUP_CH = 16
SSM_GROUPS = SSM_WIDTH // SSM_GROUP_CH
SSM_STATE = 64
DT_MIN = 0.001
DT_MAX = 0.1

IN_WIDTH = POOL_WIDTH + 2 * QK_WIDTH + ATTN_WIDTH + SSM_WIDTH
MIX_WIDTH = POOL_WIDTH + ATTN_WIDTH + SSM_WIDTH

NUM_BUCKETS = 32
MAX_EXACT = NUM_BUCKETS // 2
MAX_DISTANCE = 128

N_EXPERTS = 64
TOP_K = 8
N_EXPERT_GROUPS = 8
TOPK_GROUPS = 4
D_EXPERT = D_MODEL // 4
D_SHARED = D_EXPERT
ROUTED_SCALE = 2.5

kernel_name = 'hybrid_pool_diffattn_s5_moe_step'

def rmsnorm(x, g):
    xf = x.astype(F32)
    y = xf * lax.rsqrt(jnp.mean(xf * xf, axis=-1, keepdims=True) + EPS)
    return (y * g.astype(F32)).astype(x.dtype)

def cmul(ar, ai, br, bi):
    return ar * br - ai * bi, ar * bi + ai * br

def rel_position_bias(q_pos, k_pos, table):
    n = jnp.maximum(q_pos[:, None] - k_pos[None, :], 0)
    nf = jnp.maximum(n, 1).astype(F32)
    large = MAX_EXACT + (jnp.log(nf / MAX_EXACT) / math.log(MAX_DISTANCE / MAX_EXACT)
                         * (NUM_BUCKETS - MAX_EXACT)).astype(jnp.int32)
    large = jnp.minimum(large, NUM_BUCKETS - 1)
    bucket = jnp.where(n < MAX_EXACT, n, large)
    return jnp.moveaxis(table.astype(F32)[bucket], -1, 0)

def diff_attend(q, k, v, q_pos, k_pos, table, lam):
    s = jnp.einsum('bqhmd,bkhmd->bhmqk', q.astype(F32), k.astype(F32)) * (DIFF_HEAD_DIM ** -0.5)
    s = s + rel_position_bias(q_pos, k_pos, table)[None, :, None]
    s = jnp.where(k_pos[None, :] <= q_pos[:, None], s, -jnp.inf)
    p = jax.nn.softmax(s, axis=-1)
    w = p[:, :, 0] - lam * p[:, :, 1]
    return jnp.einsum('bhqk,bkhe->bqhe', w, v.astype(F32))

def pool_mix(u, prev, pos0, w_pool, scale):
    B, S, _ = u.shape
    ue = jnp.concatenate([prev.astype(F32), u.astype(F32)], axis=1)
    cs = jnp.cumsum(jnp.pad(ue, ((0, 0), (1, 0), (0, 0))), axis=1)
    end = cs[:, POOL_PREV + 1:]
    pos = (pos0 + jnp.arange(S)).astype(F32)
    means = []
    for g, w in enumerate(POOL_WINDOWS):
        sl = slice(g * POOL_GROUP_WIDTH, (g + 1) * POOL_GROUP_WIDTH)
        start = cs[:, POOL_PREV + 1 - w: POOL_PREV + 1 - w + S, sl]
        cnt = jnp.minimum(float(w), pos + 1.0)[None, :, None]
        means.append((end[..., sl] - start) / cnt)
    pooled = jnp.concatenate(means, axis=-1) - ue[:, POOL_PREV:]
    y = jnp.einsum('bsgc,gcd->bsgd', pooled.reshape(B, S, POOL_GROUPS, POOL_GROUP_WIDTH), w_pool.astype(F32))
    y = y.reshape(B, S, POOL_WIDTH) * scale.astype(F32)
    return y, ue[:, -POOL_PREV:].astype(u.dtype)

def ssm_mix(u, h0_re, h0_im, a_re, a_im, log_dt, b_re, b_im, c_re, c_im, d_skip, w_glu, b_glu):
    B, S, _ = u.shape
    uf = u.astype(F32).reshape(B, S, SSM_GROUPS, SSM_GROUP_CH)
    a_re = a_re.astype(F32)
    a_im = a_im.astype(F32)
    dt = jnp.exp(log_dt.astype(F32))[:, None]
    mag = jnp.exp(a_re * dt)
    abar_re, abar_im = mag * jnp.cos(a_im * dt), mag * jnp.sin(a_im * dt)
    den = a_re * a_re + a_im * a_im
    f_re = ((abar_re - 1.0) * a_re + abar_im * a_im) / den
    f_im = (abar_im * a_re - (abar_re - 1.0) * a_im) / den
    bb_re, bb_im = cmul(f_re[..., None], f_im[..., None], b_re.astype(F32), b_im.astype(F32))
    bu_re = jnp.einsum('bsgp,gnp->bsgn', uf, bb_re)
    bu_im = jnp.einsum('bsgp,gnp->bsgn', uf, bb_im)
    i0_re, i0_im = cmul(abar_re, abar_im, h0_re.astype(F32), h0_im.astype(F32))
    bu_re = bu_re.at[:, 0].add(i0_re)
    bu_im = bu_im.at[:, 0].add(i0_im)
    ar_t = jnp.broadcast_to(abar_re, bu_re.shape)
    ai_t = jnp.broadcast_to(abar_im, bu_im.shape)

    def combine(e1, e2):
        a1r, a1i, b1r, b1i = e1
        a2r, a2i, b2r, b2i = e2
        ar, ai = cmul(a2r, a2i, a1r, a1i)
        br, bi = cmul(a2r, a2i, b1r, b1i)
        return ar, ai, br + b2r, bi + b2i

    _, _, h_re, h_im = lax.associative_scan(combine, (ar_t, ai_t, bu_re, bu_im), axis=1)
    y = (jnp.einsum('bsgn,gpn->bsgp', h_re, c_re.astype(F32))
         - jnp.einsum('bsgn,gpn->bsgp', h_im, c_im.astype(F32)))
    y = y.reshape(B, S, SSM_WIDTH) + d_skip.astype(F32) * u.astype(F32)
    z = jax.nn.gelu(y)
    out = z * jax.nn.sigmoid(z @ w_glu.astype(F32) + b_glu.astype(F32))
    return out, h_re[:, -1], h_im[:, -1]

def moe_ffn(h, w_r, b_r, wg, wu, wd, sg, su, sd):
    shp = h.shape
    t = h.reshape(-1, shp[-1])
    T = t.shape[0]
    scores = jax.nn.sigmoid(jnp.dot(t, w_r).astype(F32))
    biased = scores + b_r.astype(F32)
    per_group = N_EXPERTS // N_EXPERT_GROUPS
    grp_score = lax.top_k(biased.reshape(T, N_EXPERT_GROUPS, per_group), 2)[0].sum(-1)
    _, grp_idx = lax.top_k(grp_score, TOPK_GROUPS)
    grp_mask = jax.nn.one_hot(grp_idx, N_EXPERT_GROUPS, dtype=F32).sum(1)
    exp_mask = jnp.repeat(grp_mask, per_group, axis=1)
    masked = jnp.where(exp_mask > 0, biased, -jnp.inf)
    _, idx = lax.top_k(masked, TOP_K)
    w = jnp.take_along_axis(scores, idx, axis=-1)
    w = w / jnp.sum(w, axis=-1, keepdims=True) * ROUTED_SCALE
    gates = jnp.einsum('tk,tke->te', w, jax.nn.one_hot(idx, N_EXPERTS, dtype=F32))

    def expert(acc, p):
        e_g, e_u, e_d, g = p
        a = jax.nn.silu(t @ e_g) * (t @ e_u)
        return acc + g[:, None] * (a @ e_d).astype(F32), None

    routed, _ = lax.scan(expert, jnp.zeros(t.shape, F32), (wg, wu, wd, gates.T))
    shared = (jax.nn.silu(t @ sg) * (t @ su)) @ sd
    return (routed + shared.astype(F32)).astype(h.dtype).reshape(shp)

def setup_inputs(seed: int = 0) -> dict:
    key = jax.random.key(seed)
    ks = iter(jax.random.split(key, 64))

    def nrm(shape, scale):
        return jax.random.normal(next(ks), shape, F32) * scale

    n_pages = PAST_LEN // PAGE_SIZE
    n_used = DEC_BATCH * n_pages
    n_phys = n_used + n_used // 4 + 1
    page_table = jax.random.permutation(next(ks), n_phys)[:n_used].reshape(DEC_BATCH, n_pages).astype(jnp.int32)
    qk = 2 * DIFF_HEAD_DIM
    return {
        'x_prompt': nrm((BATCH, SEQ, D_MODEL), 1.0),
        'x_sample': nrm((DEC_BATCH, DEC_SEQ, D_MODEL), 1.0),
        'cache_k': nrm((n_phys, DEPTH, PAGE_SIZE, DIFF_HEADS, qk), 1.0),
        'cache_v': nrm((n_phys, DEPTH, PAGE_SIZE, DIFF_HEADS, DIFF_V_DIM), 1.0),
        'state_pool': nrm((DEC_BATCH, DEPTH, POOL_PREV, POOL_WIDTH), 1.0),
        'state_ssm_re': nrm((DEC_BATCH, DEPTH, SSM_GROUPS, SSM_STATE), 0.1),
        'state_ssm_im': nrm((DEC_BATCH, DEPTH, SSM_GROUPS, SSM_STATE), 0.1),
        'page_table': page_table,
        'c_prompt': nrm((BATCH, D_MODEL), 1.0),
        'c_sample': nrm((DEC_BATCH, D_MODEL), 1.0),
        'rel_bias': nrm((NUM_BUCKETS, DIFF_HEADS), 0.5),
        'w_ada': nrm((DEPTH, D_MODEL, 6 * D_MODEL), 0.5 * D_MODEL ** -0.5),
        'b_ada': nrm((DEPTH, 6 * D_MODEL), 0.02),
        'norm1_g': 1.0 + nrm((DEPTH, D_MODEL), 0.05),
        'norm2_g': 1.0 + nrm((DEPTH, D_MODEL), 0.05),
        'final_g': 1.0 + nrm((D_MODEL,), 0.05),
        'w_in': nrm((DEPTH, D_MODEL, IN_WIDTH), D_MODEL ** -0.5),
        'w_out': nrm((DEPTH, MIX_WIDTH, D_MODEL), MIX_WIDTH ** -0.5),
        'pool_w': nrm((DEPTH, POOL_GROUPS, POOL_GROUP_WIDTH, POOL_GROUP_WIDTH), POOL_GROUP_WIDTH ** -0.5),
        'pool_scale': 1.0 + nrm((DEPTH, POOL_WIDTH), 0.1),
        'lam_q1': nrm((DEPTH, DIFF_HEAD_DIM), 0.1),
        'lam_k1': nrm((DEPTH, DIFF_HEAD_DIM), 0.1),
        'lam_q2': nrm((DEPTH, DIFF_HEAD_DIM), 0.1),
        'lam_k2': nrm((DEPTH, DIFF_HEAD_DIM), 0.1),
        'subln_g': 1.0 + nrm((DEPTH, DIFF_V_DIM), 0.05),
        'ssm_a_re': -0.5 + nrm((DEPTH, SSM_GROUPS, SSM_STATE), 0.01),
        'ssm_a_im': math.pi * jnp.arange(SSM_STATE, dtype=F32) + nrm((DEPTH, SSM_GROUPS, SSM_STATE), 0.01),
        'ssm_log_dt': jax.random.uniform(next(ks), (DEPTH, SSM_GROUPS), F32, math.log(DT_MIN), math.log(DT_MAX)),
        'ssm_b_re': nrm((DEPTH, SSM_GROUPS, SSM_STATE, SSM_GROUP_CH), (2 * SSM_GROUP_CH) ** -0.5),
        'ssm_b_im': nrm((DEPTH, SSM_GROUPS, SSM_STATE, SSM_GROUP_CH), (2 * SSM_GROUP_CH) ** -0.5),
        'ssm_c_re': nrm((DEPTH, SSM_GROUPS, SSM_GROUP_CH, SSM_STATE), (2 * SSM_STATE) ** -0.5),
        'ssm_c_im': nrm((DEPTH, SSM_GROUPS, SSM_GROUP_CH, SSM_STATE), (2 * SSM_STATE) ** -0.5),
        'ssm_d': nrm((DEPTH, SSM_WIDTH), 1.0),
        'glu_w': nrm((DEPTH, SSM_WIDTH, SSM_WIDTH), SSM_WIDTH ** -0.5),
        'glu_b': nrm((DEPTH, SSM_WIDTH), 0.02),
        'router_w': nrm((DEPTH, D_MODEL, N_EXPERTS), D_MODEL ** -0.5),
        'router_bias': nrm((DEPTH, N_EXPERTS), 0.01),
        'exp_w_gate': nrm((DEPTH, N_EXPERTS, D_MODEL, D_EXPERT), D_MODEL ** -0.5),
        'exp_w_up': nrm((DEPTH, N_EXPERTS, D_MODEL, D_EXPERT), D_MODEL ** -0.5),
        'exp_w_down': nrm((DEPTH, N_EXPERTS, D_EXPERT, D_MODEL), D_EXPERT ** -0.5),
        'shared_w_gate': nrm((DEPTH, D_MODEL, D_SHARED), D_MODEL ** -0.5),
        'shared_w_up': nrm((DEPTH, D_MODEL, D_SHARED), D_MODEL ** -0.5),
        'shared_w_down': nrm((DEPTH, D_SHARED, D_MODEL), D_SHARED ** -0.5),
    }

def reference(x_prompt, x_sample, cache_k, cache_v, state_pool, state_ssm_re, state_ssm_im, page_table,
              c_prompt, c_sample, rel_bias, w_ada, b_ada, norm1_g, norm2_g, final_g, w_in, w_out,
              pool_w, pool_scale, lam_q1, lam_k1, lam_q2, lam_k2, subln_g,
              ssm_a_re, ssm_a_im, ssm_log_dt, ssm_b_re, ssm_b_im, ssm_c_re, ssm_c_im, ssm_d, glu_w, glu_b,
              router_w, router_bias, exp_w_gate, exp_w_up, exp_w_down,
              shared_w_gate, shared_w_up, shared_w_down):
    past_len = page_table.shape[1] * cache_k.shape[2]

    def prompt_attention(q, k, v, lam, l):
        B, S = q.shape[:2]
        nb = S // Q_BLOCK
        q_blocks = jnp.moveaxis(q.reshape(B, nb, Q_BLOCK, DIFF_HEADS, 2, DIFF_HEAD_DIM), 1, 0)
        pos = jnp.arange(S, dtype=jnp.int32)
        o = lax.map(lambda blk: diff_attend(blk[0], k, v, blk[1], pos, rel_bias, lam),
                    (q_blocks, pos.reshape(nb, Q_BLOCK)))
        return jnp.moveaxis(o, 0, 1).reshape(B, S, DIFF_HEADS, DIFF_V_DIM)

    def sample_attention(q, k, v, lam, l):
        B, S = q.shape[:2]
        k_past = cache_k[page_table, l].reshape(B, past_len, DIFF_HEADS, 2, DIFF_HEAD_DIM)
        v_past = cache_v[page_table, l].reshape(B, past_len, DIFF_HEADS, DIFF_V_DIM)
        k_all = jnp.concatenate([k_past.astype(k.dtype), k], axis=1)
        v_all = jnp.concatenate([v_past.astype(v.dtype), v], axis=1)
        q_pos = past_len + jnp.arange(S, dtype=jnp.int32)
        k_pos = jnp.arange(past_len + S, dtype=jnp.int32)
        return diff_attend(q, k_all, v_all, q_pos, k_pos, rel_bias, lam)

    def layer(x, c, l, pos0, attention, pool_prev, h0_re, h0_im):
        B, S, _ = x.shape
        mod = jnp.dot(jax.nn.silu(c), w_ada[l]) + b_ada[l]
        sh1, sc1, g1, sh2, sc2, g2 = [m[:, None, :] for m in jnp.split(mod, 6, axis=-1)]
        h = rmsnorm(x, norm1_g[l]) * (1.0 + sc1) + sh1
        proj = h @ w_in[l]
        cuts = [POOL_WIDTH, POOL_WIDTH + QK_WIDTH, POOL_WIDTH + 2 * QK_WIDTH,
                POOL_WIDTH + 2 * QK_WIDTH + ATTN_WIDTH]
        u_pool, q, k, v, u_ssm = jnp.split(proj, cuts, axis=-1)
        y_a, pool_new = pool_mix(u_pool, pool_prev, pos0, pool_w[l], pool_scale[l])
        lam_init = 0.8 - 0.6 * math.exp(-0.3 * l)
        lam = (jnp.exp(jnp.sum(lam_q1[l] * lam_k1[l]).astype(F32))
               - jnp.exp(jnp.sum(lam_q2[l] * lam_k2[l]).astype(F32)) + lam_init)
        q = q.reshape(B, S, DIFF_HEADS, 2, DIFF_HEAD_DIM)
        k = k.reshape(B, S, DIFF_HEADS, 2, DIFF_HEAD_DIM)
        v = v.reshape(B, S, DIFF_HEADS, DIFF_V_DIM)
        o = attention(q, k, v, lam, l)
        y_b = (rmsnorm(o, subln_g[l]) * (1.0 - lam_init)).reshape(B, S, ATTN_WIDTH)
        y_c, h_re, h_im = ssm_mix(u_ssm, h0_re, h0_im, ssm_a_re[l], ssm_a_im[l], ssm_log_dt[l],
                                  ssm_b_re[l], ssm_b_im[l], ssm_c_re[l], ssm_c_im[l], ssm_d[l],
                                  glu_w[l], glu_b[l])
        mix = jnp.concatenate([y_a, y_b, y_c], axis=-1).astype(x.dtype)
        x = x + g1 * (mix @ w_out[l])
        h2 = rmsnorm(x, norm2_g[l]) * (1.0 + sc2) + sh2
        x = x + g2 * moe_ffn(h2, router_w[l], router_bias[l], exp_w_gate[l], exp_w_up[l], exp_w_down[l],
                             shared_w_gate[l], shared_w_up[l], shared_w_down[l])
        return (x, k.reshape(B, S, DIFF_HEADS, 2 * DIFF_HEAD_DIM), v, pool_new,
                h_re.astype(state_ssm_re.dtype), h_im.astype(state_ssm_im.dtype))

    bp = x_prompt.shape[0]
    zero_pool = jnp.zeros((bp, POOL_PREV, POOL_WIDTH), x_prompt.dtype)
    zero_h = jnp.zeros((bp, SSM_GROUPS, SSM_STATE), F32)
    xp = x_prompt
    p_new = ([], [], [], [], [])
    for l in range(DEPTH):
        xp, *st = layer(xp, c_prompt, l, 0, prompt_attention, zero_pool, zero_h, zero_h)
        for acc, s in zip(p_new, st):
            acc.append(s)
    y_prompt = rmsnorm(xp, final_g)

    xs = x_sample
    s_new = ([], [], [], [], [])
    for l in range(DEPTH):
        xs, *st = layer(xs, c_sample, l, past_len, sample_attention, state_pool[:, l],
                        state_ssm_re[:, l], state_ssm_im[:, l])
        for acc, s in zip(s_new, st):
            acc.append(s)
    y_sample = rmsnorm(xs, final_g)

    k_prompt = jnp.stack(p_new[0], axis=1)
    v_prompt = jnp.stack(p_new[1], axis=1)
    pool_prompt = jnp.stack(p_new[2], axis=1)
    ssm_re_prompt = jnp.stack(p_new[3], axis=1)
    ssm_im_prompt = jnp.stack(p_new[4], axis=1)
    k_sample = jnp.stack(s_new[0], axis=1)
    v_sample = jnp.stack(s_new[1], axis=1)
    pool_sample = jnp.stack(s_new[2], axis=1)
    ssm_re_sample = jnp.stack(s_new[3], axis=1)
    ssm_im_sample = jnp.stack(s_new[4], axis=1)
    return (y_prompt, y_sample, k_prompt, v_prompt, pool_prompt, ssm_re_prompt, ssm_im_prompt,
            k_sample, v_sample, pool_sample, ssm_re_sample, ssm_im_sample)


_drawn_inputs = setup_inputs


def setup_inputs(seed=0):
    import zlib

    import numpy as np

    out = dict(_drawn_inputs(seed))
    spreads = {}
    factors = {'lam_q1': 2.969, 'ssm_a_re': 58.651, 'ssm_c_re': 3.166, 'glu_b': 17.539, 'ssm_c_im': 6.97}
    for name, (base, spread) in spreads.items():
        noise = np.random.default_rng([zlib.crc32(name.encode()), seed]).standard_normal(out[name].shape)
        drawn = base * np.exp(spread * noise) if base else spread * noise
        out[name] = __import__('jax').numpy.asarray(drawn.astype(out[name].dtype))
    for name, factor in factors.items():
        out[name] = (out[name] * factor).astype(out[name].dtype)
    return out
```

```python
import math

import numpy as np

import concourse.bass as bass
from concourse import mybir

F32 = mybir.dt.float32
I32 = mybir.dt.int32
ACT = mybir.ActivationFunctionType
ALU = mybir.AluOpType
AX = mybir.AxisListType

P = 128
D = 1024
KD = D // P
DEPTH = 2
NP_ = 256
NS = 8
T = NP_ + NS
NC = 1 + NS
EPS = 1e-6

POOL_W, HEADS, HD, VD = 256, 4, 64, 128
WINDOWS = (2, 4, 8, 16)
PREV = 15
ATT_W = HEADS * VD
IN_W = 2048
C_POOL, C_Q, C_K, C_V, C_U = 0, 2, 6, 10, 14
PROJ = IN_W // P

SG, SN, SCH = 16, 64, 16
SC = SG * SN // P
PAST, PAGE = 256, 128
PAGES = PAST // PAGE
ROWS = NS * HEADS * 2

NE, TOPK, NG, TOPG = 64, 8, 8, 4
PG = NE // NG
DE = 256
SCALE_R = 2.5

SEG = 2048
ADA_SEGS, IN_SEGS, OUT_SEGS = 6 * D // 256, IN_W // 256, D // 256
WIDE_ADA, WIDE_IN = ADA_SEGS // 2, IN_SEGS // 2
WIDE_OUT = WIDE_ADA + WIDE_IN
WIDE_SHARED = WIDE_OUT + 1
WIDE_EXP = WIDE_SHARED + 1
WIDE_FILLS = WIDE_EXP + NE
NARROW_SHARED = OUT_SEGS - 1
NARROW_EXP = NARROW_SHARED + 1
NARROW_FILLS = NARROW_EXP + NE
assert WIDE_FILLS % 2 == 0 and NARROW_FILLS % 2 == 0 and WIDE_EXP % 2 == 0 and NARROW_EXP % 2 == 0

NEG = -1e30
ROUND = 12582912.0
TWO_PI_A = 6.28125
TWO_PI_B = 2 * math.pi - 6.28125

R_BADA, R_N1, R_N2, R_PS, R_SD, R_GB, R_SUB, R_AR, R_AI = 0, 48, 56, 64, 66, 68, 70, 71, 79
R_ALL = R_AI + SC

BUCKET_COLS = NP_ + P + 1
K_ID = 0
K_INV = K_ID + P
K_T = K_INV + 2 * NP_
K_HALF = K_T + NP_
K_LOW = K_HALF + 2
K_CMB = K_LOW + NG * NG
K_M0 = K_CMB + NS * HEADS
K_M1 = K_M0 + 1
K_AB = K_M1 + 1
K_BKT = K_AB + NS
K_LAM = K_BKT + PAST + 1
K_ONE = K_LAM + 2 * DEPTH
K_END = K_ONE + P


def shape_constants():
    c = np.zeros((P, K_END), np.float32)
    c[:, K_ID:K_ID + P] = np.eye(P)
    t = np.arange(NP_)
    for half in range(4):
        rows = slice(64 * (half % 2), 64 * (half % 2) + 64)
        cols = slice(K_INV + NP_ * (half // 2), K_INV + NP_ * (half // 2) + NP_)
        c[rows, cols] = 1.0 / np.minimum(WINDOWS[half], t + 1)
    c[:, K_T:K_T + NP_] = t
    for h in range(2):
        c[64 * h:64 * h + 64, K_HALF + h] = 1.0
    low = np.arange(NG)[None, :] < np.arange(NG)[:, None]
    c[:, K_LOW:K_LOW + NG * NG] = low.reshape(-1)
    row = np.arange(ROWS)
    c[row, K_CMB + row // 2] = 1.0
    c[row, K_M0] = row % 2 == 0
    c[row, K_M1] = row % 2 == 1
    c[row, K_AB + row // (2 * HEADS)] = 1.0
    n = np.arange(PAST + 1)
    large = 16 + (np.log(np.maximum(n, 1).astype(np.float32) / 16) / math.log(8.0) * 16).astype(np.int32)
    bucket = np.where(n < 16, n, np.minimum(large, 31))
    c[bucket, K_BKT + PAST - n] = 1.0
    for l in range(DEPTH):
        init = 0.8 - 0.6 * math.exp(-0.3 * l)
        c[:, K_LAM + 2 * l] = init
        c[:, K_LAM + 2 * l + 1] = 1.0 - init
    c[:, K_ONE:K_ONE + P] = 1.0
    return c


class Signal:

    def __init__(self, sem, per_layer):
        self.sem, self.per_layer = sem, per_layer

    def by(self, layer, k):
        return layer * self.per_layer + k


class Links:

    def __init__(self, eng, sem, per_layer):
        self.eng, self.sem, self.per_layer = eng, sem, per_layer
        self.before, self.made, self.layer = 0, 0, None

    def enter(self, layer):
        self.before, self.made, self.layer = self.made, 0, layer

    def check(self):
        assert self.made == self.per_layer, (self.made, self.per_layer)

    def leave(self):
        self.made, self.layer = self.before + DEPTH * self.per_layer, None

    def __call__(self, ins):
        self.made += 1
        ins.then_inc(self.sem, 1)
        at = self.made if self.layer is None else self.layer * self.per_layer + self.before + self.made
        self.eng.wait_ge(self.sem, at)


def program(nc, a, out):
    ctx_list = []

    def keep(cm):
        ctx_list.append(cm)
        return cm.__enter__()

    def sb(name, shape, dt=F32):
        return keep(nc.sbuf_tensor(name, shape, dt))

    def sem(name):
        return keep(nc.semaphore(name))

    def sig(name, per_layer):
        return Signal(sem(name), per_layer)

    cst = sb("cst", [P, K_END])
    xT = sb("xT", [P, KD, T])
    hT = sb("hT", [P, KD, T])
    projT = sb("projT", [P, PROJ, T])
    mixT = sb("mixT", [P, KD, T])
    wide = sb("wide", [P, 2, 2, SEG])
    narrow = sb("narrow", [P, 2, SEG])
    kbuf = sb("kbuf", [P, 2, PAGES, 512])
    vbuf = sb("vbuf", [P, 4, PAGES, 512])
    cosT = sb("cosT", [P, SC, NP_])
    sinT = sb("sinT", [P, SC, NP_])
    oT = sb("oT", [P, HEADS, T])
    rowsP = sb("rowsP", [P, 4, 512])
    biasT = sb("biasT", [P, HEADS, NP_])
    biasS = sb("biasS", [ROWS, PAST + 1])
    scratch = sb("scratch", [P, 4224])
    prow = sb("prow", [R_ALL, P])
    hrow = sb("hrow", [P, P])
    pT = sb("pT", [P, R_ALL])
    h0T = sb("h0T", [P, 2, NS, SC])
    dtall = sb("dtall", [P, SG])
    bst = sb("bst", [P, 2, SC, SCH])
    crow = sb("crow", [P, 2, 2, SN])
    bpad = sb("bpad", [P, 2, SC, 2, SCH])
    bbT = sb("bbT", [P, 2, 2, P])
    cT = sb("cT", [P, 2, 2, P])
    gluw = sb("gluw", [P, 2, 256])
    rw = sb("rw", [P, KD, NE])
    rbias = sb("rbias", [P, NE])
    poolw = sb("poolw", [P, 2, P])
    prevrow = sb("prevrow", [NS * PREV, POOL_W])
    ueS = sb("ueS", [P, 2, NS, PREV + 1])
    lamv = sb("lamv", [P, 4, HD])
    modT = sb("modT", [P, 48, NC])
    scA = sb("scA", [P, 2, KD, NC])
    condT = sb("condT", [P, KD, NC])
    finalg = sb("finalg", [P, KD])
    rowsS = sb("rowsS", [NS, 14 * P])
    poolrow = sb("poolrow", [PREV, POOL_W])
    w32 = sb("w32", [P, PAGES, NS, NS * HEADS])
    relb = sb("relb", [32, HEADS])
    relbs = sb("relbs", [32, NS, HEADS, 2])
    decS = sb("decS", [P, PAGES, ROWS])
    prodm = sb("prodm", [P, NS, HEADS, 2])
    qk = sb("qk", [P, NS, HEADS])
    comb = sb("comb", [ROWS, NS * HEADS])
    aps = sb("aps", [ROWS, NS])
    wself = sb("wself", [NS, NS * HEADS])
    sm = sb("sm", [P, 64])
    sp_ = sb("sp_", [P, 24, SC])
    i0 = sb("i0", [P, 2, SC, NS])
    i0t = sb("i0t", [P, 2, SC, NS])
    stF = sb("stF", [P, 2, SC])
    stS = sb("stS", [P, 2, NS, SC])
    strow = sb("strow", [P, 2, P])
    rstd = sb("rstd", [P, T])
    scr = sb("scr", [P, 3, NE])
    g1 = sb("g1", [P, 3, NG])
    rank = sb("rank", [P, 3, NG])
    t8 = sb("t8", [P, 3, 8])
    gsum = sb("gsum", [P, 3])
    tick_p = sb("tick_p", [1, 24])
    tick_v = sb("tick_v", [1, 8])
    ticks = [0, 0]
    ps = keep(nc.psum_tensor("ps", [P, 8, 512], F32))

    skew = nc.dram_tensor("skew", (HEADS * P * BUCKET_COLS,), F32, kind="Internal").ap()

    ident = cst[:, K_ID:K_ID + P]
    ones = cst[:, K_ONE:K_ONE + P]
    half = cst[:, K_HALF:K_HALF + 2]
    xrows = projT[:, :, :].rearrange("p a b -> p (a b)")[:, 0:4 * D].rearrange("p (a b) -> p a b", a=4)
    skews = scratch[:, 0:HEADS * BUCKET_COLS].rearrange("p (h i) -> p h i", h=HEADS)
    modrow = scratch[0:NC, 0:1024].rearrange("p (a b) -> p a b", a=2)
    ang = scratch[:, 1024:1024 + 4 * 512].rearrange("p (a j t) -> p a j t", a=4, j=2)
    prod = scratch[:, 0:1024].rearrange("p (g n) -> p g n", g=PAGES)
    od = scratch[0:NS * HEADS, 1024:1536]
    sbuf_s = scratch[:, 0:1024].rearrange("p (n m k) -> p n m k", n=2, m=2)
    sbuf_p = scratch[:, 1024:2048].rearrange("p (n m k) -> p n m k", n=2, m=2)
    sbuf_w = scratch[:, 2048:2560].rearrange("p (n k) -> p n k", n=2)
    sbuf_w0 = scratch[:, 2560:2816]
    sbuf_wT = scratch[:, 2816:3840].rearrange("p (n k q) -> p n k q", n=2, k=2)
    osq = scratch[:, 0:HEADS * T].rearrange("p (h t) -> p h t", h=HEADS)
    osd = scratch[:, HEADS * T:2 * HEADS * T].rearrange("p (h t) -> p h t", h=HEADS)
    rot = scratch[:, 0:3072].rearrange("p (a j t) -> p a j t", a=6, j=2)
    hs = scratch[:, 3072:3072 + 4 * T].rearrange("p (r j t) -> p r j t", r=2, j=2)
    yv = scratch[:, 0:2 * T].rearrange("p (a t) -> p a t", a=2)
    zv = scratch[:, 2 * T:4 * T].rearrange("p (a t) -> p a t", a=2)
    gv = scratch[:, 4 * T:6 * T].rearrange("p (a t) -> p a t", a=2)
    bb = scratch[:, 3072:3328].rearrange("p (r k c) -> p r k c", r=2, k=SC)
    crow2 = scratch[:, 3328:3840].rearrange("p (r t n) -> p r t n", r=2, t=2)
    pe64 = scratch[0:ROWS, 1536:1536 + PAST + 1]
    selb = oT[0:NS, :, :].rearrange("p a b -> p (a b)")[:, 0:NS * P].rearrange("p (b q) -> p b q", b=NS)
    relbw = mixT[0:32, :, :].rearrange("p a b -> p (a b)")[:, 0:HEADS * P].rearrange("p (h q) -> p h q", h=HEADS)
    hflat = hT[:, :, :].rearrange("p a b -> p (a b)")
    span = 2 * (PREV + NP_)
    ue, win_a, win_b = (hflat[:, n * span:(n + 1) * span].rearrange("p (c t) -> p c t", c=2) for n in range(3))
    pooled = mixT[:, 0:2, :]
    silu = scratch[:, 0:4 * T].rearrange("p (n f t) -> p n f t", n=2, f=2)
    act = scratch[:, 4 * T:8 * T].rearrange("p (n f t) -> p n f t", n=2, f=2)
    scT = scratch[0:NE, 8 * T:9 * T]
    acc = projT[:, 0:KD, :]
    cflat = cosT[:, :, :].rearrange("p a b -> p (a b)")
    gT = cflat[0:NE, 0:T]
    gd = cflat[0:NE, T:3 * T].rearrange("p (n t) -> p n t", n=2)
    biased = cflat[:, 800:992].rearrange("p (t e) -> p t e", t=3)
    masked = cflat[:, 992:1184].rearrange("p (t e) -> p t e", t=3)
    pairs = cflat[:, 1184:1376].rearrange("p (t g e) -> p t g e", t=3, g=NG)
    pairs2 = cflat[:, 1376:1568].rearrange("p (t g e) -> p t g e", t=3, g=NG)
    g8 = cflat[:, 1568:1760].rearrange("p (t g e) -> p t g e", t=3, g=NG)

    start_loaded = sem("start_loaded")
    start_ready = sem("start_ready")
    start_copied_v = sem("start_copied_v")
    start_copied_a = sem("start_copied_a")
    start_vector = sem("start_vector")
    start_silu = sem("start_silu")
    skew_moved = sem("skew_moved")
    wide_free, wide_loaded = sem("wide_free"), [sem("wide_loaded0"), sem("wide_loaded1")]
    narrow_free, narrow_loaded = sem("narrow_free"), [sem("narrow_loaded0"), sem("narrow_loaded1")]
    params_free = sem("params_free")
    N_PARAM = 33
    params_loaded = sig("params_loaded", 16 * N_PARAM)
    rows_turned = sig("rows_turned", 1)
    rows_copied = sig("rows_copied", 1)
    prev_copied = sig("prev_copied", 1)
    crow_ready = sig("crow_ready", 1)
    c_turned = sig("c_turned", 1)
    bpad_ready = sig("bpad_ready", 1)
    b_turned = sig("b_turned", 1)
    cb_copied = sig("cb_copied", 2)
    dt_ready = sig("dt_ready", 1)
    mag_in = sig("mag_in", 1)
    mag_ready = sig("mag_ready", 1)
    angle_ready = sig("angle_ready", 1 + SC // 2)
    sines_ready = sig("sines_ready", 1 + SC // 2)
    lam_sums = sig("lam_sums", 1)
    lam_exp = sig("lam_exp", 1)
    ada_made = sig("ada_made", 12)
    ada_copied = sig("ada_copied", 12)
    ada_turned = sig("ada_turned", 12)
    mod_ready = sig("mod_ready", 1)
    squares = sig("squares", 2)
    sumsq = sig("sumsq", 2)
    var_ready = sig("var_ready", 2)
    sd_ready = sig("sd_ready", 2)
    h_ready = sig("h_ready", 2)
    proj_made = sig("proj_made", PROJ)
    proj_copied_a = sig("proj_copied_a", PROJ // 2)
    proj_copied_v = sig("proj_copied_v", PROJ // 2)
    srows_made = sig("srows_made", 1)
    srows_copied = sig("srows_copied", 1)
    prows_made = sig("prows_made", 1)
    prows_copied = sig("prows_copied", 1)
    k_loaded = [sig(f"k_loaded{n}", 16 * PAGES * NS // 2) for n in range(2)]
    v_loaded = [sig(f"v_loaded{n}", 16 * PAGES * NS // 4) for n in range(4)]
    q_spread = sig("q_spread", NS)
    dec_products = sig("dec_products", NS)
    dec_scored = sig("dec_scored", 1)
    dec_turned = sig("dec_turned", 1)
    dec_max = sig("dec_max", 1)
    dec_exp = sig("dec_exp", 1)
    comb_ready = sig("comb_ready", 1)
    dec_weights = sig("dec_weights", 1)
    w32_ready = sig("w32_ready", 1)
    dec_pv = sig("dec_pv", NS)
    dec_o_copied = sig("dec_o_copied", 1)
    dec_o_turned = sig("dec_o_turned", 1)
    scored = sig("scored", 2 * HEADS)
    biased_ready = sig("biased_ready", 2 * HEADS)
    negmax = sig("negmax", 2 * HEADS)
    probs = sig("probs", 2 * HEADS)
    w_ready = sig("w_ready", 2 * HEADS)
    w_turned = sig("w_turned", 2 * HEADS)
    w_copied = sig("w_copied", 2 * HEADS)
    pv_made = sig("pv_made", HEADS)
    pv_copied = sig("pv_copied", HEADS)
    o_ready = sig("o_ready", 1)
    o_squared = sig("o_squared", 1)
    o_sums = sig("o_sums", 1)
    o_var = sig("o_var", 1)
    o_sd = sig("o_sd", 1)
    attn_mixed = sig("attn_mixed", 1)
    pool_sample = sig("pool_sample", 1)
    pool_prompt = sig("pool_prompt", 1)
    pool_made = sig("pool_made", 2)
    pool_mixed = sig("pool_mixed", 2)
    bu_made = sig("bu_made", SC // 2)
    bu_used = sig("bu_used", SC // 2)
    hs_ready = sig("hs_ready", SC // 2)
    y_made = sig("y_made", SC // 2)
    y_ready = sig("y_ready", 1)
    gelu_ready = sig("gelu_ready", 1)
    glu_made = sig("glu_made", 1)
    glu_gate = sig("glu_gate", 1)
    ssm_mixed = sig("ssm_mixed", 1)
    st_ready = sig("st_ready", 1)
    st_turned = sig("st_turned", 1)
    st_copied = sig("st_copied", 1)
    out_made = sig("out_made", KD)
    out_added = sig("out_added", KD)
    logits = sig("logits", 1)
    scores_sig = sig("scores_sig", 1)
    scores_turned = sig("scores_turned", 1)
    gates_ready = sig("gates_ready", 1)
    gates_turned = sig("gates_turned", 1)
    acc_zero = sig("acc_zero", 1)
    ge_ready = sig("ge_ready", NE + 1)
    act_gated = sig("act_gated", NE + 1)
    gu_made = sig("gu_made", NE + 1)
    silu_ready = sig("silu_ready", NE + 1)
    act_ready = sig("act_ready", NE + 1)
    down_made = sig("down_made", KD * (NE + 1))
    down_added = sig("down_added", KD * (NE + 1))
    x_ready = sig("x_ready", 1)
    cache_stored = sem("cache_stored")
    stores = sem("stores")
    N_STORE = 4 + 1 + 3 + NS + 2 + 2 * NS
    last = {k: sem("last_" + k) for k in ("squares", "sumsq", "var", "sd", "h", "turned", "copied")}
    vlink, alink, plink = sem("vector_link"), sem("scalar_link"), sem("pool_link")
    layer_stores = Signal(stores, 16 * N_STORE)

    block = keep(nc.Block())

    def wide_at(layer, f):
        return wide_loaded[f % 2], 32 * (layer * (WIDE_FILLS // 2) + f // 2 + 1)

    def narrow_at(layer, f):
        return narrow_loaded[f % 2], 16 * (layer * (NARROW_FILLS // 2) + f // 2 + 1)

    @block.sync
    def _(sp):
        def columns(w, s):
            return w[:, 256 * s:256 * s + 256].rearrange("(k p) n -> p k n", p=P)

        def seg(t):
            return t.rearrange("p (k n) -> p k n", k=KD)

        sp.sem_inc(wide_free, 2)
        sp.sem_inc(narrow_free, 2)
        with sp.Fori(0, DEPTH) as layer:
            ada, win, wout = a["w_ada"][layer], a["w_in"][layer], a["w_out"][layer]
            for f in range(WIDE_OUT):
                w, s = (ada, 2 * f) if f < WIDE_ADA else (win, 2 * (f - WIDE_ADA))
                sp.wait_ge(wide_free, layer * WIDE_FILLS + f + 1)
                for j in range(2):
                    sp.dma_start(seg(wide[:, f % 2, j]), columns(w, s + j)).then_inc(wide_loaded[f % 2], 16)
            sp.wait_ge(wide_free, layer * WIDE_FILLS + WIDE_OUT + 1)
            for j in range(2):
                sp.dma_start(seg(wide[:, WIDE_OUT % 2, 0])[:, 4 * j:4 * j + 4],
                             columns(wout, 0)[:, 4 * j:4 * j + 4]).then_inc(wide_loaded[WIDE_OUT % 2], 16)
            for f in range(NARROW_SHARED):
                sp.wait_ge(narrow_free, layer * NARROW_FILLS + f + 1)
                sp.dma_start(seg(narrow[:, f % 2]), columns(wout, f + 1)).then_inc(narrow_loaded[f % 2], 16)

            def expert(g, u, d, fw, fn, slot):
                sp.wait_ge(wide_free, layer * WIDE_FILLS + fw + 1)
                for j, w in enumerate((g, u)):
                    sp.dma_start(seg(wide[:, slot, j]), w.rearrange("(k p) n -> p k n", p=P)).then_inc(wide_loaded[slot], 16)
                sp.wait_ge(narrow_free, layer * NARROW_FILLS + fn + 1)
                sp.dma_start(narrow[:, slot].rearrange("p (k n) -> p k n", k=2),
                             d.rearrange("(k p) n -> p k n", p=P)).then_inc(narrow_loaded[slot], 16)

            expert(a["shared_w_gate"][layer], a["shared_w_up"][layer], a["shared_w_down"][layer],
                   WIDE_SHARED, NARROW_SHARED, 1)
            wg, wu, wd = (a[n].rearrange("l (e j) r c -> (l e) j r c", j=2) for n in ("exp_w_gate", "exp_w_up", "exp_w_down"))
            with sp.Fori(0, NE // 2) as pair:
                for j in range(2):
                    e, e0 = layer * (NE // 2) + pair, 2 * pair
                    expert(wg[e, j], wu[e, j], wd[e, j], WIDE_EXP + e0 + j, NARROW_EXP + e0 + j, j)

    @block.gpsimd
    def _(pool):
        gp = nc.gpsimd

        def load(sem_, dst, src):
            pool.dma_start(dst, src, allow_slow_non_contiguous=True).then_inc(sem_, 16)

        load(start_loaded, cst[:, :], a["consts"])
        for t in range(2):
            load(start_loaded, xrows[:, t, :], a["x_prompt"][0, P * t:P * t + P, :])
        load(start_loaded, xrows[0:NS, 2, :], a["x_sample"][:, 0, :])
        load(start_loaded, xrows[0:1, 3, :], a["c_prompt"])
        load(start_loaded, xrows[1:NC, 3, :], a["c_sample"])
        load(start_loaded, relb[:, :], a["rel_bias"])
        load(start_loaded, hrow[0:KD, :], a["final_g"].rearrange("(k p) -> k p", p=P))
        chain = Links(pool, plink, 9)

        def held():
            ticks[0] += 1
            gp.tensor_tensor(tick_p[:, ticks[0] - 1:ticks[0]], cst[0:1, K_ONE:K_ONE + 1], cst[0:1, K_ONE:K_ONE + 1], ALU.add)

        gp.memset(poolw[:, :, :], 0.0)
        gp.memset(w32[:, :, :, :], 0.0)
        gp.memset(skews[:, :, PAST + 1:], NEG)
        chain(gp.memset(scr[:, :, :], 0.0))
        before = chain.made
        pool.wait_ge(start_copied_a, 4)
        load(skew_moved, skew.rearrange("(h p i) -> p h i", h=HEADS, p=P), skews)
        pool.wait_ge(skew_moved, 16)
        for h in range(HEADS):
            src = bass.AP(skew.tensor, h * P * BUCKET_COLS + P, [[BUCKET_COLS - 1, P], [1, NP_]])
            load(skew_moved, biasT[:, h, :], src)

        kc, vc = a["cache_k"], a["cache_v"]
        pt = sb("pt", [1, NS * PAGES], I32)
        load(start_loaded, pt[:, :], a["page_table"].rearrange("b n -> (b n)")[None, :])
        pool.wait_ge(start_loaded, 16 * 9)
        pool.wait_ge(start_vector, 2)
        pages = [pool.value_load(pt[0:1, n:n + 1], min_val=0, max_val=kc.shape[0] - 1) for n in range(NS * PAGES)]
        kcf = kc.rearrange("n l t h d -> (n l) t (h d)")
        vcf = vc.rearrange("n l t h d -> (n l) t (h d)")
        pool.sem_inc(cache_stored, 1)
        with pool.Fori(0, DEPTH) as layer:
            chain.enter(layer)
            pool.wait_ge(params_free, layer + 1)
            n0 = [0]

            def par(dst, src):
                n0[0] += 1
                load(params_loaded.sem, dst, src)

            def rows(v):
                return v.rearrange("(k p) -> k p", p=P)

            par(prow[R_BADA:R_BADA + 48, :], rows(a["b_ada"][layer]))
            par(prow[R_N1:R_N1 + 8, :], rows(a["norm1_g"][layer]))
            par(prow[R_N2:R_N2 + 8, :], rows(a["norm2_g"][layer]))
            par(prow[R_PS:R_PS + 2, :], rows(a["pool_scale"][layer]))
            par(prow[R_SD:R_SD + 2, :], rows(a["ssm_d"][layer]))
            par(prow[R_GB:R_GB + 2, :], rows(a["glu_b"][layer]))
            par(prow[R_SUB:R_SUB + 1, :], rows(a["subln_g"][layer]))
            par(prow[R_AR:R_AR + 8, :], a["ssm_a_re"][layer].rearrange("(k g) n -> k (g n)", g=2))
            par(prow[R_AI:R_AI + 8, :], a["ssm_a_im"][layer].rearrange("(k g) n -> k (g n)", g=2))
            par(dtall[:, :], a["ssm_log_dt"][layer].partition_broadcast(P))
            for r, name in enumerate(("state_ssm_re", "state_ssm_im")):
                v = a[name].rearrange("b l (k g) n -> l b k (g n)", g=2)[layer]
                for q in range(2):
                    par(hrow[64 * r + 32 * q:64 * r + 32 * q + 32, :], v[4 * q:4 * q + 4])
            for r, name in enumerate(("ssm_b_re", "ssm_b_im")):
                par(bst[:, r], a[name][layer].rearrange("(k g) n c -> (g n) k c", g=2))
            for r, name in enumerate(("ssm_c_re", "ssm_c_im")):
                par(crow[:, r], a[name][layer].rearrange("(t g) c n -> (g c) t n", t=2))
            par(gluw[:, :, :], a["glu_w"][layer].rearrange("(k p) n -> p k n", p=P))
            par(rw[:, :, :], a["router_w"][layer].rearrange("(k p) n -> p k n", p=P))
            par(rbias[:, :], a["router_bias"][layer].partition_broadcast(P))
            for n, name in enumerate(("lam_q1", "lam_k1", "lam_q2", "lam_k2")):
                par(lamv[:, n, :], a[name][layer].partition_broadcast(P))
            for g in range(4):
                r0 = 64 * (g % 2)
                par(poolw[r0:r0 + 64, g // 2, r0:r0 + 64], a["pool_w"][layer, g])
            for b in range(NS):
                if b % 2 == 0:
                    par(prevrow[PREV * b:PREV * b + 2 * PREV, :], a["state_pool"].rearrange("b l t c -> l b t c")[layer, b:b + 2])
            assert n0[0] == N_PARAM, n0

            def load_k(b):
                for g in range(PAGES):
                    load(k_loaded[b % 2].sem, kbuf[:, b % 2, g, :], kcf[pages[b * PAGES + g] * DEPTH + layer])

            def load_v(b):
                for g in range(PAGES):
                    load(v_loaded[b % 4].sem, vbuf[:, b % 4, g, :], vcf[pages[b * PAGES + g] * DEPTH + layer])

            for b in range(2):
                load_k(b)
            for b in range(4):
                load_v(b)
            for b in range(2, NS):
                pool.wait_ge(dec_products.sem, dec_products.by(layer, b - 1))
                held()
                load_k(b)

            def store(dst, src):
                st[0] += 1
                pool.dma_start(dst, src, allow_slow_non_contiguous=True).then_inc(stores, 16)

            st = [0]
            pool.wait_ge(prows_copied.sem, prows_copied.by(layer, 1))
            held()
            for n, name in enumerate(("k_prompt", "v_prompt")):
                o = out[name].rearrange("b l s h d -> b l s (h d)")
                for t in range(2):
                    store(o[0, layer, P * t:P * t + P, :], rowsP[:, 2 * n + t, :])
            store(out["pool_prompt"][0, layer], poolrow[:, :])
            pool.wait_ge(srows_copied.sem, srows_copied.by(layer, 1))
            held()
            store(out["k_sample"].rearrange("b l s h d -> l b (s h d)")[layer], rowsS[:, 512:1024])
            store(out["v_sample"].rearrange("b l s h d -> l b (s h d)")[layer], rowsS[:, 1024:1536])
            ps_o = out["pool_sample"].rearrange("b l t c -> l b t c")
            store(ps_o[layer, :, PREV - 1, :], rowsS[:, 1536:1792])
            pool.wait_ge(params_loaded.sem, params_loaded.by(layer, 16 * N_PARAM))
            held()
            for b in range(NS):
                store(ps_o[layer, b, 0:PREV - 1, :], prevrow[PREV * b + 1:PREV * b + PREV, :])

            pool.wait_ge(proj_made.sem, proj_made.by(layer, PROJ))
            pool.wait_ge(proj_copied_a.sem, proj_copied_a.by(layer, 1))
            pool.wait_ge(proj_copied_v.sem, proj_copied_v.by(layer, 1))
            held()
            gp.memset(ue[:, :, 0:PREV], 0.0)
            chain(gp.tensor_copy(ue[:, :, PREV:], projT[:, C_POOL:C_POOL + 2, 0:NP_]))
            inv = cst[:, K_INV:K_INV + 2 * NP_].rearrange("p (c t) -> p c t", c=2)
            source = ue
            L = PREV + NP_
            for n, w in enumerate(WINDOWS):
                dest = (win_a, win_b)[n % 2]
                lo, s = w - 1, w // 2
                chain(gp.tensor_tensor(dest[:, :, lo:L], source[:, :, lo:L], source[:, :, lo - s:L - s], ALU.add))
                rows_, c = slice(64 * (n % 2), 64 * (n % 2) + 64), n // 2
                chain(gp.tensor_tensor(pooled[rows_, c, 0:NP_], dest[rows_, c, PREV:], inv[rows_, c, :], ALU.mult))
                source = dest
            gp.tensor_tensor(pooled[:, :, 0:NP_], pooled[:, :, 0:NP_], ue[:, :, PREV:], ALU.subtract)\
                .then_inc(pool_prompt.sem, 1)

            for b in range(4, NS):
                pool.wait_ge(dec_pv.sem, dec_pv.by(layer, b - 3))
                held()
                load_v(b)

            pool.wait_ge(st_copied.sem, st_copied.by(layer, 1))
            held()
            for r, name in enumerate(("ssm_re_prompt", "ssm_im_prompt")):
                store(out[name][0, layer].rearrange("(k g) n -> k (g n)", g=2), strow[SC * r:SC * r + SC, 0, :])
            for r, name in enumerate(("ssm_re_sample", "ssm_im_sample")):
                o = out[name].rearrange("b l (k g) n -> l b k (g n)", g=2)[layer]
                for b in range(NS):
                    store(o[b], strow[64 * r + SC * b:64 * r + SC * b + SC, 1, :])
            pool.wait_ge(out_made.sem, out_made.by(layer, KD))
            pool.wait_ge(ssm_mixed.sem, ssm_mixed.by(layer, 1))
            held()
            gp.memset(acc, 0.0).then_inc(acc_zero.sem, 1)
            pool.wait_ge(stores, layer_stores.by(layer, 16 * st[0]))
            pool.sem_inc(cache_stored, 1)
            assert chain.made == chain.per_layer and 16 * st[0] == layer_stores.per_layer, (chain.made, st)
        yrows = projT[:, :, :].rearrange("p a b -> p (a b)")[:, 0:3 * D].rearrange("p (a b) -> p a b", a=3)
        pool.wait_ge(last["copied"], 6)
        for t in range(2):
            pool.dma_start(out["y_prompt"][0, P * t:P * t + P, :], yrows[:, t, :]).then_inc(stores, 16)
        pool.dma_start(out["y_sample"][:, 0, :], yrows[0:NS, 2, :]).then_inc(stores, 16)
        pool.wait_ge(stores, DEPTH * layer_stores.per_layer + 48)

    @block.tensor
    def _(pe):
        mm = nc.tensor.matmul

        def turn(dst, src, n):
            return nc.tensor.transpose(dst, src, ident[0:n, 0:n])

        def times_one(dst, src, n):
            return mm(dst, src, ident[0:n, 0:n], start=True, stop=True)

        pe.wait_ge(start_loaded, 16 * 8)
        for k in range(KD):
            if k >= 4:
                pe.wait_ge(start_copied_v, k - 3)
            for t in range(3):
                n = P if t < 2 else NS
                ins = turn(ps[:, k % 4, P * t:P * t + n], xrows[0:n, t, P * k:P * k + P], n)
            ins.then_inc(start_ready, 1)
        pe.wait_ge(start_vector, 1)
        for h in range(HEADS):
            mm(ps[:, 4 + h, 0:PAST + 1], relbw[:, h, :], cst[0:32, K_BKT:K_BKT + PAST + 1],
               start=True, stop=True).then_inc(start_ready, 1)
        pe.wait_ge(start_copied_v, 8)
        pe.wait_ge(start_silu, 1)
        for k in range(KD):
            turn(ps[:, 0, NC * k:NC * k + NC], xrows[0:NC, 3, P * k:P * k + P], NC)
        turn(ps[:, 1, 0:KD], hrow[0:KD, :], KD)
        mm(ps[0:ROWS, 2, 0:PAST + 1], relbs[:, :, :, :].rearrange("p a b c -> p (a b c)"),
           cst[0:32, K_BKT:K_BKT + PAST + 1], start=True, stop=True).then_inc(start_ready, 1)

        def sum_squares(bank, done):
            for k in range(KD):
                ins = mm(ps[:, bank, 0:T], ones, hT[:, k, :], start=k == 0, stop=k == KD - 1)
            ins.then_inc(done, 1)

        pe.wait_ge(start_vector, 2)
        with pe.Fori(0, DEPTH) as layer:
            def W(s, k=1):
                pe.wait_ge(s.sem, s.by(layer, k))

            W(x_ready)
            W(params_loaded, 16 * N_PARAM)
            turn(ps[:, 4, 0:R_ALL], prow[:, :], R_ALL)
            turn(ps[:, 4, P:2 * P], hrow[:, :], P)
            for c in range(2):
                ins = turn(ps[:, 5, P * c:P * c + NS * PREV], prevrow[:, P * c:P * c + P], NS * PREV)
            ins.then_inc(rows_turned.sem, 1)

            def ada_turn(q, frees=False):
                pe.wait_ge(ada_copied.sem, ada_copied.by(layer, q + 1))
                for j in range(4):
                    ins = times_one(ps[:, 2, NC * (4 * q + j):NC * (4 * q + j) + NC],
                                    modrow[:, q % 2, P * j:P * j + P], NC)
                    if frees and j == 0:
                        ins.then_inc(wide_free, 1)
                ins.then_inc(ada_turned.sem, 1)

            for q in range(WIDE_ADA):
                if q >= 2:
                    W(ada_copied, q - 1)
                pe.wait_ge(*wide_at(layer, q))
                for j in range(2):
                    seg = wide[:, q % 2, j].rearrange("p (k n) -> p k n", k=KD)
                    for k in range(KD):
                        ins = mm(ps[0:NC, q % 2, 256 * j:256 * j + 256], condT[:, k, :], seg[:, k, :],
                                 start=k == 0, stop=k == KD - 1, skip_group_check=True)
                        if q >= 1 and j + k == 0:
                            ins.then_inc(wide_free, 1)
                ins.then_inc(ada_made.sem, 1)
                if q >= 1:
                    ada_turn(q - 1)
            ada_turn(WIDE_ADA - 1, True)

            W(crow_ready)
            for r in range(2):
                for t in range(2):
                    ins = turn(ps[:, 6, P * (2 * r + t):P * (2 * r + t) + P], crow2[:, r, t, :], P)
            ins.then_inc(c_turned.sem, 1)
            W(bpad_ready)
            for r in range(2):
                for t in range(2):
                    ins = turn(ps[:, 7, P * (2 * r + t):P * (2 * r + t) + P],
                               bpad[:, r, 4 * t:4 * t + 4].rearrange("p k h c -> p (k h c)"), P)
            ins.then_inc(b_turned.sem, 1)

            W(squares, 1)
            sum_squares(3, sumsq.sem)

            W(h_ready, 1)
            for c in range(PROJ):
                s, f = c // 2, WIDE_ADA + c // 4
                if c % 4 == 0:
                    pe.wait_ge(*wide_at(layer, f))
                if c >= 4:
                    W((proj_copied_a, proj_copied_v)[c % 2], (c - 4) // 2 + 1)
                w = wide[:, f % 2, s % 2].rearrange("p (k n) -> p k n", k=KD)
                for k in range(KD):
                    ins = mm(ps[:, c % 4, 0:T], w[:, k, P * (c % 2):P * (c % 2) + P], hT[:, k, :],
                             start=k == 0, stop=k == KD - 1)
                    if c >= 4 and c % 4 == 0 and k == 0:
                        ins.then_inc(wide_free, 1)
                ins.then_inc(proj_made.sem, 1)

            W(proj_copied_a, PROJ // 2)
            W(proj_copied_v, PROJ // 2)
            W(cb_copied, 2)
            for n, c in enumerate([*range(C_Q, C_Q + 12), 0, 1]):
                ins = turn(ps[0:NS, 4 + n // 4, P * (n % 4):P * (n % 4) + P], projT[:, c, NP_:T], P)
                if n == 0:
                    ins.then_inc(wide_free, 1)
            ins.then_inc(srows_made.sem, 1)
            for n, c0 in enumerate((C_K, C_V)):
                for t in range(2):
                    for h in range(HEADS):
                        turn(ps[:, 2 * n + t, P * h:P * h + P], projT[:, c0 + h, P * t:P * t + P], P)
            W(srows_copied)
            for c in range(2):
                ins = turn(ps[0:PREV, 7, 256 + P * c:256 + P * c + P], projT[:, c, NP_ - PREV:NP_], P)
            ins.then_inc(prows_made.sem, 1)

            for b in range(NS):
                if b >= 2:
                    W(dec_products, b - 1)
                mm(ps[:, 4 + b % 2, :], selb[:, b, :], rowsS[:, 0:512], start=True, stop=True)\
                    .then_inc(q_spread.sem, 1)
            pe.wait_ge(dec_scored.sem, dec_scored.by(layer, 1))
            for g in range(PAGES):
                times_one(ps[0:ROWS, 6, P * g:P * g + P], decS[:, g, :], P)
            mm(ps[0:ROWS, 6, PAST:PAST + 1], prodm[:, :, :, :].rearrange("p a b c -> p (a b c)"), ones[:, 0:1],
               start=True, stop=True).then_inc(dec_turned.sem, 1)
            W(comb_ready)
            W(prows_copied)
            for g in range(PAGES):
                mm(ps[:, 7, 32 * g:32 * g + 32], pe64[:, P * g:P * g + P], comb[:, :], start=True, stop=True)
            mm(ps[0:NS, 7, 64:96], aps[:, :], comb[:, :], start=True, stop=True).then_inc(dec_weights.sem, 1)
            W(w32_ready)
            W(dec_products, NS)
            for b in range(NS):
                pe.wait_ge(v_loaded[b % 4].sem, v_loaded[b % 4].by(layer, 32 * (b // 4 + 1)))
                for g in range(PAGES):
                    ins = mm(ps[0:32, 5, :], w32[:, g, b, :], vbuf[:, b % 4, g, :], start=b + g == 0, stop=False)
                if b == NS - 1:
                    ins = mm(ps[0:32, 5, :], wself[:, :], rowsS[:, 1024:1536], start=False, stop=True)
                ins.then_inc(dec_pv.sem, 1)
            pe.wait_ge(dec_o_copied.sem, dec_o_copied.by(layer, 1))
            for h in range(HEADS):
                ins = times_one(ps[:, 5, 32 * h:32 * h + 32], od[:, P * h:P * h + P], 32)
            ins.then_inc(dec_o_turned.sem, 1)

            def scores(n):
                h, i = n // 2, n % 2
                keys = P * (i + 1)
                if n >= 2:
                    W(biased_ready, n - 1)
                for m in range(2):
                    rows_ = slice(HD * m, HD * m + HD)
                    ins = mm(ps[:, 2 * (n % 2) + m, 0:keys], projT[rows_, C_Q + h, P * i:P * i + P],
                             projT[rows_, C_K + h, 0:keys], start=True, stop=True, skip_group_check=True)
                ins.then_inc(scored.sem, 1)

            scores(0)
            for n in range(2 * HEADS):
                h, i = n // 2, n % 2
                if n + 1 < 2 * HEADS:
                    scores(n + 1)
                W(w_ready, n + 1)
                if n >= 2:
                    W(w_copied, n - 1)
                for t in range(i + 1):
                    ins = turn(ps[:, 6 + n % 2, P * t:P * t + P], sbuf_w[:, n % 2, P * t:P * t + P], P)
                ins.then_inc(w_turned.sem, 1)
                if i == 1:
                    W(w_copied, n + 1)
                    if h >= 1:
                        W(pv_copied, h)
                    mm(ps[:, 4, 0:NP_], rowsP[:, 2, P * h:P * h + P], sbuf_wT[:, h % 2, 0, :],
                       start=True, stop=False)
                    mm(ps[:, 4, P:NP_], rowsP[:, 3, P * h:P * h + P], sbuf_wT[:, h % 2, 1, P:NP_],
                       start=False, stop=True).then_inc(pv_made.sem, 1)
            W(o_squared)
            for h in range(HEADS):
                ins = mm(ps[:, h, 0:T], ones, osq[:, h, :], start=True, stop=True)
            ins.then_inc(o_sums.sem, 1)

            W(pool_prompt)
            W(pool_sample)
            W(o_ready)
            for c in range(2):
                mm(ps[:, 6 + c, 0:T], poolw[:, c, :], pooled[:, c, :], start=True, stop=True)\
                    .then_inc(pool_made.sem, 1)

            W(o_var)
            W(pv_copied, HEADS)

            def drive(p):
                if p >= 1:
                    W(bu_used, p)
                for r in range(2):
                    for j in range(2):
                        c = 2 * p + j
                        rows_ = slice(32 * (c % 4), 32 * (c % 4) + 32)
                        ins = mm(ps[:, 2 * r + j, 0:T], bbT[rows_, r, c // 4, :], projT[rows_, C_U + c // 4, :],
                                 start=True, stop=True, tile_position=(32 * (c % 4), 0))
                ins.then_inc(bu_made.sem, 1)

            drive(0)
            for p in range(SC // 2):
                W(hs_ready, p + 1)
                for j in range(2):
                    c = 2 * p + j
                    cols = slice(32 * (c % 4), 32 * (c % 4) + 32)
                    for r in range(2):
                        ins = mm(ps[cols, 4 + c // 4, 0:T], cT[:, r, c // 4, cols], hs[:, r, j, :],
                                 start=r == 0, stop=r == 1, skip_group_check=True,
                                 tile_position=(0, 32 * (c % 4)))
                ins.then_inc(y_made.sem, 1)
                if p + 1 < SC // 2:
                    drive(p + 1)
            W(st_ready)
            turn(ps[0:2 * SC, 0, 0:P], stF[:, :, :].rearrange("p a b -> p (a b)"), P)
            turn(ps[:, 1, 0:P], stS[:, :, :, :].rearrange("p a b c -> p (a b c)"), P).then_inc(st_turned.sem, 1)
            W(gelu_ready)
            W(pool_mixed, 2)
            for c in range(2):
                for k in range(2):
                    ins = mm(ps[:, 6 + c, 0:T], gluw[:, k, P * c:P * c + P], zv[:, k, :], start=k == 0, stop=k == 1)
            ins.then_inc(glu_made.sem, 1)

            W(attn_mixed)
            W(ssm_mixed)
            W(st_copied)
            for c in range(KD):
                s = c // 2
                if c % 2 == 0:
                    pe.wait_ge(*(wide_at(layer, WIDE_OUT) if s == 0 else narrow_at(layer, s - 1)))
                if c >= 4:
                    W(out_added, c - 3)
                w = (wide[:, WIDE_OUT % 2, 0] if s == 0 else narrow[:, (s - 1) % 2]).rearrange("p (k n) -> p k n", k=KD)
                for k in range(KD):
                    ins = mm(ps[:, c % 4, 0:T], w[:, k, P * (c % 2):P * (c % 2) + P], mixT[:, k, :],
                             start=k == 0, stop=k == KD - 1)
                    if c >= 2 and c % 2 == 0 and k == 0:
                        ins.then_inc(wide_free if s == 1 else narrow_free, 1)
                ins.then_inc(out_made.sem, 1)

            W(squares, 2)
            sum_squares(4, sumsq.sem)
            W(h_ready, 2)
            for k in range(KD):
                ins = mm(ps[0:NE, 5, 0:T], rw[:, k, :], hT[:, k, :], start=k == 0, stop=k == KD - 1)
                if k == 0:
                    ins.then_inc(narrow_free, 1)
            ins.then_inc(logits.sem, 1)
            pe.wait_ge(scores_sig.sem, scores_sig.by(layer, 1))
            for t in range(3):
                n = P if t < 2 else NS
                ins = times_one(ps[0:n, 6, NE * t:NE * t + NE], scT[:, P * t:P * t + n], NE)
            ins.then_inc(scores_turned.sem, 1)

            def gate_up(slot, at, frees):
                pe.wait_ge(*at)
                for f in range(4):
                    w = wide[:, slot, f // 2].rearrange("p (k n) -> p k n", k=KD)
                    for k in range(KD):
                        ins = mm(ps[:, f, 0:T], w[:, k, P * (f % 2):P * (f % 2) + P], hT[:, k, :],
                                 start=k == 0, stop=k == KD - 1)
                        if frees and f + k == 0:
                            ins.then_inc(frees, 1)
                return ins

            def down(slot, n, at, frees):
                pe.wait_ge(*at)
                w = narrow[:, slot].rearrange("p (k n) -> p k n", k=2)
                for c in range(KD):
                    pe.wait_ge(down_added.sem, down_added.by(layer, KD * n + max(c + 1, 3)))
                    for k in range(2):
                        ins = mm(ps[:, 5 + c % 3, 0:T], w[:, k, P * c:P * c + P], act[:, slot, k, :],
                                 start=k == 0, stop=k == 1)
                        if frees and c + k == 0:
                            ins.then_inc(frees, 1)
                    ins.then_inc(down_made.sem, 1)

            W(out_added, KD)
            gate_up(1, wide_at(layer, WIDE_SHARED), None).then_inc(gu_made.sem, 1)
            pe.wait_ge(gates_ready.sem, gates_ready.by(layer, 1))
            for t in range(3):
                n = P if t < 2 else NS
                ins = times_one(ps[0:NE, 7, P * t:P * t + n], scr[0:n, t, :], n)
                if t == 0:
                    ins.then_inc(wide_free, 1)
            ins.then_inc(gates_turned.sem, 1)
            def step(e0, j, frees_narrow):
                e = e0 + j
                pe.wait_ge(act_ready.sem, act_ready.by(layer, e + 1))
                gate_up(j, (wide_loaded[j], 32 * (layer * (WIDE_FILLS // 2) + WIDE_EXP // 2 + 1) + 16 * e0),
                        frees_narrow)
                pe.wait_ge(ge_ready.sem, ge_ready.by(layer, e + 1))
                mm(ps[:, 4, 0:T], ones[0:NE, :], gd[:, j, :], start=True, stop=True).then_inc(gu_made.sem, 1)
                down(1 - j, e, (narrow_loaded[1 - j],
                                16 * (layer * (NARROW_FILLS // 2) + NARROW_EXP // 2 + j) + 8 * e0), wide_free)

            step(0, 0, None)
            step(0, 1, narrow_free)
            with pe.Fori(2, NE, 2) as e0:
                for j in range(2):
                    step(e0, j, narrow_free)
            pe.wait_ge(act_ready.sem, act_ready.by(layer, NE + 1))
            down(1, NE, narrow_at(layer, NARROW_FILLS - 1), narrow_free)
            pe.wait_ge(down_made.sem, down_made.by(layer, KD * (NE + 1)))
            pe.sem_inc(narrow_free, 1)

        pe.wait_ge(last["squares"], 1)
        sum_squares(0, last["sumsq"])
        pe.wait_ge(last["h"], 1)
        for t in range(3):
            n = P if t < 2 else NS
            for g in range(2):
                for k in range(4):
                    ins = turn(ps[0:n, 1 + 2 * t + g, P * k:P * k + P], hT[:, 4 * g + k, P * t:P * t + n], P)
            ins.then_inc(last["turned"], 1)

    @block.scalar
    def _(se):
        act_ = nc.scalar.activation
        chain = Links(se, alink, SCALAR_LINKS)
        pe_ = start_ready
        se.wait_ge(start_loaded, 16 * 8)
        act_(xrows[0:NC, 3, :], xrows[0:NC, 3, :], ACT.Silu).then_inc(start_silu, 1)
        for h in range(HEADS):
            se.wait_ge(pe_, KD + h + 1)
            act_(skews[:, h, 0:PAST + 1], ps[:, 4 + h, 0:PAST + 1], ACT.Copy).then_inc(start_copied_a, 1)
        se.wait_ge(skew_moved, 16)
        se.wait_ge(start_vector, 2)
        quarter = sm[:, 0:1]
        with se.Fori(0, DEPTH) as layer:
            chain.enter(layer)

            def W(s, k=1):
                se.wait_ge(s.sem, s.by(layer, k))

            def ada_copy(q):
                W(ada_made, q + 1)
                if q >= 2:
                    W(ada_turned, q - 1)
                act_(modrow[:, q % 2, :], ps[0:NC, q % 2, :], ACT.Copy).then_inc(ada_copied.sem, 1)

            W(x_ready)
            act_(hT[:, :, :], xT[:, :, :], ACT.Square).then_inc(squares.sem, 1)
            W(rows_copied)
            for h in range(2):
                rows_ = slice(SN * h, SN * h + SN)
                ins = act_(sp_[rows_, 0, :], dtall[rows_, :].rearrange("p (k g) -> p g k", g=2)[:, h, :], ACT.Exp)
            ins.then_inc(dt_ready.sem, 1)
            W(mag_in)
            act_(sp_[:, 2, :], sp_[:, 1, :], ACT.Exp).then_inc(mag_ready.sem, 1)
            W(lam_sums)
            act_(sm[:, 4:6], sm[:, 2:4], ACT.Exp).then_inc(lam_exp.sem, 1)
            ada_copy(0)
            ada_copy(1)
            W(angle_ready, 1)
            act_(sp_[:, 7, :], sp_[:, 4, :], ACT.Sin)
            chain(act_(sp_[:, 11, :], sp_[:, 4, :], ACT.Abs))
            act_(sp_[:, 8, :], sp_[:, 11, :], ACT.Sin, bias=quarter, scale=-1.0).then_inc(sines_ready.sem, 1)
            for p in range(SC // 2):
                ada_copy(2 + 2 * p)
                ada_copy(3 + 2 * p)
                W(angle_ready, 2 + p)
                a0, a1 = ang[:, 2 * (p % 2)], ang[:, 2 * (p % 2) + 1]
                act_(sinT[:, 2 * p:2 * p + 2, :], a0, ACT.Sin)
                chain(act_(a1, a0, ACT.Abs))
                act_(cosT[:, 2 * p:2 * p + 2, :], a1, ACT.Sin, bias=quarter, scale=-1.0).then_inc(sines_ready.sem, 1)
            ada_copy(10)
            ada_copy(11)
            W(b_turned)
            act_(bbT[:, :, :, :].rearrange("p a b c -> p (a b c)"), ps[:, 7, :], ACT.Copy).then_inc(cb_copied.sem, 1)
            W(var_ready, 1)
            act_(rstd[:, :], rstd[:, :], ACT.Sqrt).then_inc(sd_ready.sem, 1)
            for c in range(0, PROJ, 2):
                W(proj_made, c + 1)
                act_(projT[:, c, :], ps[:, c % 4, 0:T], ACT.Copy).then_inc(proj_copied_a.sem, 1)
            se.wait_ge(cache_stored, layer + 1)
            W(srows_made)
            for n in range(4):
                m = 512 if n < 3 else 256
                ins = act_(rowsS[:, 512 * n:512 * n + m], ps[0:NS, 4 + n, 0:m], ACT.Copy)
            ins.then_inc(srows_copied.sem, 1)
            W(prows_made)
            for n in range(4):
                act_(rowsP[:, n, :], ps[:, n, :], ACT.Copy)
            act_(poolrow[:, :], ps[0:PREV, 7, 256:512], ACT.Copy).then_inc(prows_copied.sem, 1)
            W(dec_max)
            act_(pe64[:, :], pe64[:, :], ACT.Exp, bias=sm[0:ROWS, 9:10], accum_out=sm[0:ROWS, 10:11])\
                .then_inc(dec_exp.sem, 1)
            W(dec_pv, NS)
            act_(od, ps[0:32, 5, :], ACT.Copy).then_inc(dec_o_copied.sem, 1)
            W(dec_o_turned)
            def exps(n):
                keys = P * (n % 2 + 1)
                W(negmax, n + 1)
                for m in range(2):
                    ins = act_(sbuf_p[:, n % 2, m, 0:keys], sbuf_s[:, n % 2, m, 0:keys], ACT.Exp,
                               bias=sm[:, 12 + 2 * (n % 2) + m:13 + 2 * (n % 2) + m],
                               accum_out=sm[:, 16 + 2 * (n % 2) + m:17 + 2 * (n % 2) + m])
                ins.then_inc(probs.sem, 1)

            def turned(n):
                h, i = n // 2, n % 2
                W(w_turned, n + 1)
                if h >= 2:
                    W(pv_made, h - 1)
                act_(sbuf_wT[:, h % 2, 0:i + 1, P * i:P * i + P],
                     ps[:, 6 + n % 2, 0:P * (i + 1)].rearrange("p (t q) -> p t q", t=i + 1), ACT.Copy)\
                    .then_inc(w_copied.sem, 1)

            exps(0)
            for n in range(2 * HEADS):
                if n + 1 < 2 * HEADS:
                    exps(n + 1)
                turned(n)
                if n % 2 == 1:
                    h = n // 2
                    W(pv_made, h + 1)
                    act_(oT[:, h, 0:NP_], ps[:, 4, 0:NP_], ACT.Copy).then_inc(pv_copied.sem, 1)
            W(o_ready)
            W(pv_copied, HEADS)
            act_(osq, oT[:, :, :], ACT.Square).then_inc(o_squared.sem, 1)
            W(o_var)
            act_(osd, osd, ACT.Sqrt).then_inc(o_sd.sem, 1)
            for c in range(2):
                W(pool_made, c + 1)
                act_(mixT[:, c, :], ps[:, 6 + c, 0:T], ACT.Copy, scale=pT[:, R_PS + c:R_PS + c + 1]).then_inc(pool_mixed.sem, 1)
            W(st_turned)
            act_(strow[0:2 * SC, 0, :], ps[0:2 * SC, 0, 0:P], ACT.Copy)
            act_(strow[:, 1, :], ps[:, 1, 0:P], ACT.Copy).then_inc(st_copied.sem, 1)
            W(y_ready)
            act_(zv, yv, ACT.Gelu_apprx_tanh).then_inc(gelu_ready.sem, 1)
            W(glu_made)
            for c in range(2):
                ins = act_(gv[:, c, :], ps[:, 6 + c, 0:T], ACT.Sigmoid, bias=pT[:, R_GB + c:R_GB + c + 1])
            ins.then_inc(glu_gate.sem, 1)
            W(out_added, KD)
            W(pool_prompt)
            act_(hT[:, :, :], xT[:, :, :], ACT.Square).then_inc(squares.sem, 1)
            W(var_ready, 2)
            act_(rstd[:, :], rstd[:, :], ACT.Sqrt).then_inc(sd_ready.sem, 1)
            W(logits)
            W(ssm_mixed)
            act_(scT, ps[0:NE, 5, 0:T], ACT.Sigmoid).then_inc(scores_sig.sem, 1)
            W(gu_made, 1)
            act_(silu[:, 1], ps[:, 0:2, 0:T], ACT.Silu).then_inc(silu_ready.sem, 1)
            with se.Fori(0, NE, 2) as e0:
                for j in range(2):
                    se.wait_ge(gu_made.sem, gu_made.by(layer, e0 + j + 2))
                    act_(silu[:, j], ps[:, 0:2, 0:T], ACT.Silu).then_inc(silu_ready.sem, 1)
            chain.check()
        se.wait_ge(x_ready.sem, DEPTH + 1)
        act_(hT[:, :, :], xT[:, :, :], ACT.Square).then_inc(last["squares"], 1)
        se.wait_ge(last["var"], 1)
        act_(rstd[:, :], rstd[:, :], ACT.Sqrt).then_inc(last["sd"], 1)
        yrows = projT[:, :, :].rearrange("p a b -> p (a b)")[:, 0:3 * D].rearrange("p (a b) -> p a b", a=3)
        for t in range(3):
            n = P if t < 2 else NS
            se.wait_ge(last["turned"], t + 1)
            for g in range(2):
                act_(yrows[0:n, t, 512 * g:512 * g + 512], ps[0:n, 1 + 2 * t + g, :], ACT.Copy).then_inc(last["copied"], 1)

    @block.vector
    def _(dve):
        v = nc.vector
        ts, tt, stt, cp = v.tensor_scalar, v.tensor_tensor, v.scalar_tensor_tensor, v.tensor_copy
        chain = Links(dve, vlink, VECTOR_LINKS)
        v.memset(sm[:, 0:1], math.pi / 2)
        dve.wait_ge(start_loaded, 16 * 8)
        cp(relbw[:, :, :], relb[:, :].unsqueeze(2).to_broadcast([32, HEADS, P]))
        for m in range(2):
            ins = cp(relbs[:, :, :, m], relb[:, :].unsqueeze(1).to_broadcast([32, NS, HEADS]))
        ins.then_inc(start_vector, 1)
        for k in range(KD):
            dve.wait_ge(start_ready, k + 1)
            cp(xT[:, k, :], ps[:, k % 4, 0:T]).then_inc(start_copied_v, 1)
        dve.wait_ge(start_ready, KD + HEADS + 1)
        dve.wait_ge(start_copied_a, HEADS)
        cp(condT[:, :, :].rearrange("p a b -> p (a b)"), ps[:, 0, 0:KD * NC])
        cp(finalg[:, :], ps[:, 1, 0:KD])
        chain(cp(biasS[:, :], ps[0:ROWS, 2, 0:PAST + 1]))
        dve.sem_inc(params_free, 1)
        dve.sem_inc(x_ready.sem, 1)
        dve.sem_inc(down_added.sem, 3)
        dve.sem_inc(start_vector, 1)
        dve.wait_ge(skew_moved, 16 * (1 + HEADS))

        def held():
            ticks[1] += 1
            v.memset(tick_v[:, ticks[1] - 1:ticks[1]], 0.0)

        def norm(wait_sum, bank, var_done, wait_sd, A, B, done):
            wait_sum()
            ts(rstd[:, :], ps[:, bank, 0:T], 1.0 / D, EPS, ALU.mult, ALU.add).then_inc(var_done, 1)
            wait_sd()
            chain(v.reciprocal(rstd[:, :], rstd[:, :]))
            chain(tt(hT[:, :, :], xT[:, :, :], rstd[:, :].unsqueeze(1).to_broadcast([P, KD, T]), ALU.mult))
            if B is None:
                for k in range(KD):
                    ins = ts(hT[:, k, :], hT[:, k, :], A[:, k:k + 1], None, ALU.mult)
            else:
                for k in range(KD):
                    ts(hT[:, k, 0:NP_], hT[:, k, 0:NP_], A[:, k, 0:1], B[:, k, 0:1], ALU.mult, ALU.add)
                chain(tt(hT[:, :, NP_:T], hT[:, :, NP_:T], A[:, :, 1:NC], ALU.mult))
                ins = tt(hT[:, :, NP_:T], hT[:, :, NP_:T], B[:, :, 1:NC], ALU.add)
            ins.then_inc(done, 1)

        with dve.Fori(0, DEPTH) as layer:
            chain.enter(layer)

            def W(s, k=1):
                dve.wait_ge(s.sem, s.by(layer, k))

            S = lambda n: sp_[:, n, :]
            W(params_loaded, 16 * N_PARAM)
            cp(selb[:, :, :], cst[0:NS, K_ID:K_ID + NS].unsqueeze(2).to_broadcast([NS, NS, P]))
            for d in range(2):
                ins = cp(crow2[:, :, :, SN * d:SN * d + SN], crow[:, :, :, :])
            ins.then_inc(crow_ready.sem, 1)
            for n in range(2):
                chain(tt(lamv[:, 2 * n, :], lamv[:, 2 * n, :], lamv[:, 2 * n + 1, :], ALU.mult))
                ins = v.tensor_reduce(sm[:, 2 + n:3 + n], lamv[:, 2 * n, :], AX.X, ALU.add)
            ins.then_inc(lam_sums.sem, 1)
            W(rows_turned)
            cp(h0T[:, :, :, :].rearrange("p a b c -> p (a b c)"), ps[:, 4, P:2 * P])
            for c in range(2):
                cp(ueS[:, c, :, 0:PREV], ps[:, 5, P * c:P * c + NS * PREV].rearrange("p (b t) -> p b t", b=NS))
            cp(pT[:, :], ps[:, 4, 0:R_ALL]).then_inc(rows_copied.sem, 1)
            W(rows_copied)
            W(dt_ready)
            tt(S(3), pT[:, R_AI:R_AI + SC], S(0), ALU.mult)
            tt(S(1), pT[:, R_AR:R_AR + SC], S(0), ALU.mult).then_inc(mag_in.sem, 1)
            W(mag_in)
            chain(ts(S(6), S(3), 1.0 / (2 * math.pi), ROUND, ALU.mult, ALU.add))
            chain(ts(S(6), S(6), ROUND, None, ALU.subtract))
            chain(stt(S(4), S(6), -TWO_PI_A, S(3), ALU.mult, ALU.add))
            chain(stt(S(4), S(6), -TWO_PI_B, S(4), ALU.mult, ALU.add))
            ts(S(4), S(4), -3.1415925, 3.1415925, ALU.max, ALU.min).then_inc(angle_ready.sem, 1)
            W(angle_ready, 1)
            ts(S(5), S(4), 1.0 / (2 * math.pi), None, ALU.mult)
            chain(ts(S(12), S(4), ROUND / 1024, ROUND / 1024, ALU.add, ALU.subtract))
            chain(tt(S(13), S(4), S(12), ALU.subtract))
            tcol = cst[:, K_T:K_T + NP_]
            for p in range(SC // 2):
                if p >= 2:
                    W(sines_ready, p)
                a0, a1 = ang[:, 2 * (p % 2)], ang[:, 2 * (p % 2) + 1]
                for j in range(2):
                    c = 2 * p + j
                    ts(a0[:, j, :], tcol, sp_[:, 12, c:c + 1], None, ALU.mult)
                    ins = ts(a1[:, j, :], tcol, sp_[:, 5, c:c + 1], ROUND, ALU.mult, ALU.add)
                chain(ins)
                chain(ts(a1, a1, ROUND, None, ALU.subtract))
                chain(stt(a0, a1, -TWO_PI_A, a0, ALU.mult, ALU.add))
                chain(stt(a0, a1, -TWO_PI_B, a0, ALU.mult, ALU.add))
                for j in range(2):
                    c = 2 * p + j
                    ins = stt(a0[:, j, :], tcol, sp_[:, 13, c:c + 1], a0[:, j, :], ALU.mult, ALU.add)
                chain(ins)
                ts(a0, a0, -3.1415925, 3.1415925, ALU.max, ALU.min).then_inc(angle_ready.sem, 1)
                if p == 0:
                    W(sines_ready, 1)
                    W(mag_ready)
                    tt(S(9), S(2), S(8), ALU.mult)
                    tt(S(10), S(2), S(7), ALU.mult)
                    tt(S(14), pT[:, R_AR:R_AR + SC], pT[:, R_AR:R_AR + SC], ALU.mult)
                    chain(tt(S(15), pT[:, R_AI:R_AI + SC], pT[:, R_AI:R_AI + SC], ALU.mult))
                    tt(S(14), S(14), S(15), ALU.add)
                    chain(ts(S(16), S(9), 1.0, None, ALU.subtract))
                    v.reciprocal(S(14), S(14))
                    tt(S(17), S(16), pT[:, R_AR:R_AR + SC], ALU.mult)
                    tt(S(18), S(10), pT[:, R_AI:R_AI + SC], ALU.mult)
                    tt(S(19), S(10), pT[:, R_AR:R_AR + SC], ALU.mult)
                    chain(tt(S(20), S(16), pT[:, R_AI:R_AI + SC], ALU.mult))
                    tt(S(17), S(17), S(18), ALU.add)
                    chain(tt(S(19), S(19), S(20), ALU.subtract))
                    tt(S(17), S(17), S(14), ALU.mult)
                    chain(tt(S(19), S(19), S(14), ALU.mult))
                    wide_ = lambda s: s.unsqueeze(2).to_broadcast([P, SC, SCH])
                    tt(bpad[:, 0, :, 0, :], bst[:, 0], wide_(S(17)), ALU.mult)
                    tt(bpad[:, 0, :, 1, :], bst[:, 1], wide_(S(19)), ALU.mult)
                    tt(bpad[:, 1, :, 0, :], bst[:, 1], wide_(S(17)), ALU.mult)
                    chain(tt(bpad[:, 1, :, 1, :], bst[:, 0], wide_(S(19)), ALU.mult))
                    tt(bb[:, 0], bpad[:, 0, :, 0, :], bpad[:, 0, :, 1, :], ALU.subtract)
                    chain(tt(bb[:, 1], bpad[:, 1, :, 0, :], bpad[:, 1, :, 1, :], ALU.add))
                    for r in range(2):
                        for h in range(2):
                            ins = ts(bpad[:, r, :, h, :], bb[:, r], half[:, h:h + 1], None, ALU.mult)
                    ins.then_inc(bpad_ready.sem, 1)
                    wide_ = lambda s: s.unsqueeze(2).to_broadcast([P, SC, NS])
                    h0 = [h0T[:, r].rearrange("p b k -> p k b") for r in range(2)]
                    tt(i0[:, 0], h0[0], wide_(S(9)), ALU.mult)
                    tt(i0t[:, 0], h0[1], wide_(S(10)), ALU.mult)
                    tt(i0[:, 1], h0[1], wide_(S(9)), ALU.mult)
                    chain(tt(i0t[:, 1], h0[0], wide_(S(10)), ALU.mult))
                    tt(i0[:, 0], i0[:, 0], i0t[:, 0], ALU.subtract)
                    tt(i0[:, 1], i0[:, 1], i0t[:, 1], ALU.add)
                    W(lam_exp)
                    chain(tt(sm[:, 6:7], sm[:, 5:6], sm[:, 4:5], ALU.subtract))
                    tt(sm[:, 6:7], sm[:, 6:7], cst[:, bass.ds(K_LAM + 2 * layer, 1)], ALU.subtract)
                    chain(tt(sm[:, 7:8], pT[:, R_SUB:R_SUB + 1], cst[:, bass.ds(K_LAM + 1 + 2 * layer, 1)], ALU.mult))
            neglam = sm[:, 6:7]
            W(c_turned)
            for r in range(2):
                for h in range(2):
                    src = ps[:, 6, 256 * r:256 * r + 256].rearrange("p (t k h c) -> p t k h c", t=2, k=4, h=2)[:, :, :, h, :]
                    dst = cT[:, r].rearrange("p t (k h c) -> p t k h c", k=4, h=2)[:, :, :, h, :]
                    for t in range(2):
                        ins = ts(dst[:, t], src[:, t], half[:, h:h + 1], -1.0 if r else 1.0, ALU.mult, ALU.mult)
            ins.then_inc(cb_copied.sem, 1)
            W(ada_turned, WIDE_ADA)
            tt(modT[:, :, :], ps[:, 2, 0:48 * NC].rearrange("p (a b) -> p a b", b=NC),
               pT[:, R_BADA:R_BADA + 48].unsqueeze(2).to_broadcast([P, 48, NC]), ALU.add).then_inc(mod_ready.sem, 1)
            W(mod_ready)
            for n, (c, r) in enumerate(((8, R_N1), (32, R_N2))):
                chain(ts(scA[:, n], modT[:, c:c + 8, :], 1.0, None, ALU.add))
                chain(tt(scA[:, n], scA[:, n], pT[:, r:r + 8].unsqueeze(2).to_broadcast([P, KD, NC]), ALU.mult))
            norm(lambda: W(sumsq, 1), 3, var_ready.sem, lambda: W(sd_ready, 1), scA[:, 0], modT[:, 0:8, :], h_ready.sem)

            for c in range(1, PROJ, 2):
                W(proj_made, c + 1)
                cp(projT[:, c, :], ps[:, c % 4, 0:T]).then_inc(proj_copied_v.sem, 1)
            W(proj_copied_v, PROJ // 2)
            W(proj_copied_a, PROJ // 2)
            W(sines_ready, 1 + SC // 2)
            for c in range(2):
                ins = cp(ueS[:, c, :, PREV], projT[:, c, NP_:T])
            chain(ins)
            for n, w in enumerate(WINDOWS):
                rows_, c = slice(64 * (n % 2), 64 * (n % 2) + 64), n // 2
                ins = v.tensor_reduce(pooled[rows_, c, NP_:T], ueS[rows_, c, :, PREV + 1 - w:], AX.X, ALU.add)
            chain(ins)
            for n, w in enumerate(WINDOWS):
                rows_, c = slice(64 * (n % 2), 64 * (n % 2) + 64), n // 2
                ins = ts(pooled[rows_, c, NP_:T], pooled[rows_, c, NP_:T], 1.0 / w, None, ALU.mult)
            chain(ins)
            tt(pooled[:, :, NP_:T], pooled[:, :, NP_:T], projT[:, 0:2, NP_:T], ALU.subtract).then_inc(pool_sample.sem, 1)

            qs = projT[:, C_Q:C_Q + HEADS, NP_:T].rearrange("p h b -> p b h")
            ks = projT[:, C_K:C_K + HEADS, NP_:T].rearrange("p h b -> p b h")
            chain(tt(qk[:, :, :], qs, ks, ALU.mult))
            for m in range(2):
                ts(prodm[:, :, :, m], qk[:, :, :], half[:, m:m + 1], None, ALU.mult)
            for b in range(NS):
                W(q_spread, b + 1)
                dve.wait_ge(k_loaded[b % 2].sem, k_loaded[b % 2].by(layer, 32 * (b // 2 + 1)))
                for g in range(PAGES):
                    ins = tt(prod[:, g, :], ps[:, 4 + b % 2, :], kbuf[:, b % 2, g, :], ALU.mult)
                ins.then_inc(dec_products.sem, 1)
                W(dec_products, b + 1)
                ins = v.tensor_reduce(decS[:, :, 8 * b:8 * b + 8], prod.rearrange("p g (a d) -> p g a d", d=HD), AX.X, ALU.add)
                if b == NS - 1:
                    ins.then_inc(dec_scored.sem, 1)
                else:
                    chain(ins)
            W(dec_turned)
            chain(stt(pe64[:, :], ps[0:ROWS, 6, 0:PAST + 1], HD ** -0.5, biasS[:, :], ALU.mult, ALU.add))
            chain(v.reduce_max(sm[0:ROWS, 8:9], pe64[:, :], AX.X))
            ts(sm[0:ROWS, 9:10], sm[0:ROWS, 8:9], -1.0, None, ALU.mult).then_inc(dec_max.sem, 1)
            W(dec_exp)
            v.reciprocal(sm[0:ROWS, 11:12], sm[0:ROWS, 10:11])
            chain(stt(sm[0:ROWS, 8:9], cst[0:ROWS, K_M1:K_M1 + 1], sm[0:ROWS, 6:7], cst[0:ROWS, K_M0:K_M0 + 1], ALU.mult, ALU.add))
            ts(aps[:, :], cst[0:ROWS, K_AB:K_AB + NS], pe64[:, PAST:PAST + 1], None, ALU.mult)
            ts(comb[:, :], cst[0:ROWS, K_CMB:K_CMB + 32], sm[0:ROWS, 8:9], sm[0:ROWS, 11:12], ALU.mult, ALU.mult)\
                .then_inc(comb_ready.sem, 1)
            W(dec_weights)
            cp(wself[:, :], ps[0:NS, 7, 64:96])
            for g in range(PAGES):
                for b in range(NS):
                    ins = cp(w32[:, g, b, 4 * b:4 * b + 4], ps[:, 7, 32 * g + 4 * b:32 * g + 4 * b + 4])
            ins.then_inc(w32_ready.sem, 1)

            def biased_scores(n):
                h, i = n // 2, n % 2
                keys = P * (i + 1)
                W(scored, n + 1)
                if n >= 2:
                    W(probs, n - 1)
                s = sbuf_s[:, n % 2, :, 0:keys]
                stt(s, ps[:, 2 * (n % 2):2 * (n % 2) + 2, 0:keys], HD ** -0.5,
                    biasT[:, h, NP_ - keys:NP_].unsqueeze(1).to_broadcast([P, 2, keys]), ALU.mult, ALU.add)\
                    .then_inc(biased_ready.sem, 1)
                W(biased_ready, n + 1)
                mx = sm[:, 20 + 2 * (n % 2):22 + 2 * (n % 2)]
                chain(v.tensor_reduce(mx, s, AX.X, ALU.max))
                ts(sm[:, 12 + 2 * (n % 2):14 + 2 * (n % 2)], mx, -1.0, None, ALU.mult).then_inc(negmax.sem, 1)

            def weights(n):
                keys = P * (n % 2 + 1)
                W(probs, n + 1)
                if n >= 2:
                    W(w_turned, n - 1)
                p_ = sbuf_p[:, n % 2]
                rs = sm[:, 24:26]
                chain(v.reciprocal(rs, sm[:, 16 + 2 * (n % 2):18 + 2 * (n % 2)]))
                tt(sm[:, 26:27], rs[:, 1:2], neglam, ALU.mult)
                chain(ts(sbuf_w0[:, 0:keys], p_[:, 0, 0:keys], rs[:, 0:1], None, ALU.mult))
                stt(sbuf_w[:, n % 2, 0:keys], p_[:, 1, 0:keys], sm[:, 26:27], sbuf_w0[:, 0:keys], ALU.mult, ALU.add)\
                    .then_inc(w_ready.sem, 1)

            biased_scores(0)
            for n in range(2 * HEADS):
                if n + 1 < 2 * HEADS:
                    biased_scores(n + 1)
                weights(n)
            W(dec_o_turned)
            for h in range(HEADS):
                ins = cp(oT[:, h, NP_:T], ps[:, 5, 32 * h:32 * h + 32].rearrange("p (b h) -> p h b", h=HEADS)[:, h, :])
            ins.then_inc(o_ready.sem, 1)
            W(w_ready, 2 * HEADS)
            W(o_sums)
            ts(osd, ps[:, 0:HEADS, 0:T], 1.0 / VD, EPS, ALU.mult, ALU.add).then_inc(o_var.sem, 1)
            W(o_sd)
            W(pv_copied, HEADS)
            W(o_ready)
            chain(v.reciprocal(osd, osd))
            chain(tt(osd, osd, oT[:, :, :], ALU.mult))
            ts(mixT[:, 2:6, :], osd, sm[:, 7:8], None, ALU.mult).then_inc(attn_mixed.sem, 1)
            W(attn_mixed)

            for p in range(SC // 2):
                W(bu_made, p + 1)
                if p >= 1:
                    W(y_made, p)
                C, Sn = cosT[:, 2 * p:2 * p + 2, :], sinT[:, 2 * p:2 * p + 2, :]
                br, bi = ps[:, 0:2, 0:NP_], ps[:, 2:4, 0:NP_]
                R = lambda n: rot[:, n]
                tt(R(0), C, br, ALU.mult)
                tt(R(1), Sn, bi, ALU.mult)
                tt(R(2), C, bi, ALU.mult)
                chain(tt(R(3), Sn, br, ALU.mult))
                for r in range(2):
                    ins = tt(hs[:, r, :, NP_:T], ps[:, 2 * r:2 * r + 2, NP_:T], i0[:, r, 2 * p:2 * p + 2, :], ALU.add)
                ins.then_inc(bu_used.sem, 1)
                tt(R(0), R(0), R(1), ALU.add)
                chain(tt(R(2), R(2), R(3), ALU.subtract))
                for j in range(2):
                    mag = sp_[:, 2, 2 * p + j:2 * p + j + 1].to_broadcast([P, NP_])
                    v.tensor_tensor_scan(R(4)[:, j, :], mag, R(0)[:, j, :], 0.0, ALU.mult, ALU.add)
                    ins = v.tensor_tensor_scan(R(5)[:, j, :], mag, R(2)[:, j, :], 0.0, ALU.mult, ALU.add)
                chain(ins)
                tt(R(0), C, R(4), ALU.mult)
                tt(R(1), Sn, R(5), ALU.mult)
                tt(R(2), Sn, R(4), ALU.mult)
                chain(tt(R(3), C, R(5), ALU.mult))
                tt(hs[:, 0, :, 0:NP_], R(0), R(1), ALU.subtract)
                tt(hs[:, 1, :, 0:NP_], R(2), R(3), ALU.add).then_inc(hs_ready.sem, 1)
                W(hs_ready, p + 1)
                for r in range(2):
                    cp(stF[:, r, 2 * p:2 * p + 2], hs[:, r, :, NP_ - 1])
                    ins = cp(stS[:, r, :, 2 * p:2 * p + 2], hs[:, r, :, NP_:T].rearrange("p k b -> p b k"))
                if p == SC // 2 - 1:
                    ins.then_inc(st_ready.sem, 1)
            W(y_made, SC // 2)
            W(st_ready)
            for c in range(2):
                ins = stt(yv[:, c, :], projT[:, C_U + c, :], pT[:, R_SD + c:R_SD + c + 1], ps[:, 4 + c, 0:T], ALU.mult, ALU.add)
            ins.then_inc(y_ready.sem, 1)
            W(glu_gate)
            tt(mixT[:, 6:8, :], zv, gv, ALU.mult).then_inc(ssm_mixed.sem, 1)

            for c in range(KD):
                W(out_made, c + 1)
                g = modT[:, 16 + c, :]
                tt(sm[:, 32 + 8 * (c % 2):40 + 8 * (c % 2)], ps[:, c % 4, NP_:T], g[:, 1:NC], ALU.mult)
                chain(stt(xT[:, c, 0:NP_], ps[:, c % 4, 0:NP_], g[:, 0:1], xT[:, c, 0:NP_], ALU.mult, ALU.add))
                tt(xT[:, c, NP_:T], xT[:, c, NP_:T], sm[:, 32 + 8 * (c % 2):40 + 8 * (c % 2)], ALU.add).then_inc(out_added.sem, 1)
            W(out_added, KD)
            norm(lambda: W(sumsq, 2), 4, var_ready.sem, lambda: W(sd_ready, 2), scA[:, 1], modT[:, 24:32, :], h_ready.sem)

            W(scores_turned)
            cp(scr[:, 0:2, :], ps[:, 6, 0:2 * NE].rearrange("p (t e) -> p t e", t=2))
            chain(cp(scr[0:NS, 2, :], ps[0:NS, 6, 2 * NE:3 * NE]))
            chain(tt(biased[:, :, :], scr[:, :, :], rbias[:, :].unsqueeze(1).to_broadcast([P, 3, NE]), ALU.add))
            held()
            for t in range(3):
                for g in range(NG):
                    ins = v.max(g8[:, t, g, :], biased[:, t, PG * g:PG * g + PG])
            chain(ins)
            chain(tt(g1[:, :, :], g8[:, :, :, 0], g8[:, :, :, 1], ALU.add))
            low = cst[:, K_LOW:K_LOW + NG * NG].rearrange("p (i j) -> p i j", i=NG)
            for t in range(3):
                me = g1[:, t, :].unsqueeze(2).to_broadcast([P, NG, NG])
                other = g1[:, t, :].unsqueeze(1).to_broadcast([P, NG, NG])
                tt(pairs[:, t], other, me, ALU.is_gt)
                ins = tt(pairs2[:, t], other, me, ALU.is_equal)
            chain(ins)
            for t in range(3):
                ins = tt(pairs2[:, t], pairs2[:, t], low, ALU.mult)
            chain(ins)
            chain(tt(pairs[:, :, :, :], pairs[:, :, :, :], pairs2[:, :, :, :], ALU.add))
            chain(v.tensor_reduce(rank[:, :, :], pairs[:, :, :, :], AX.X, ALU.add))
            chain(ts(rank[:, :, :], rank[:, :, :], float(TOPG), NEG, ALU.is_ge, ALU.mult))
            chain(tt(masked[:, :, :].rearrange("p t (g e) -> p (t g) e", g=NG), biased[:, :, :].rearrange("p t (g e) -> p (t g) e", g=NG),
                     rank[:, :, :].rearrange("p t g -> p (t g)").unsqueeze(2).to_broadcast([P, 3 * NG, PG]), ALU.add))
            held()
            for t in range(3):
                ins = v.max(t8[:, t, :], masked[:, t, :])
            chain(ins)
            held()
            for t in range(3):
                ins = v.match_replace(masked[:, t, :], t8[:, t, :], masked[:, t, :], 3 * NEG)
            chain(ins)
            chain(ts(masked[:, :, :], masked[:, :, :], 2 * NEG, None, ALU.is_le))
            chain(tt(scr[:, :, :], scr[:, :, :], masked[:, :, :], ALU.mult))
            chain(v.tensor_reduce(gsum[:, :], scr[:, :, :], AX.X, ALU.add))
            chain(ts(gsum[:, :], gsum[:, :], 1e-30, None, ALU.max))
            chain(v.reciprocal(gsum[:, :], gsum[:, :]))
            for t in range(3):
                ins = ts(scr[:, t, :], scr[:, t, :], gsum[:, t:t + 1], SCALE_R, ALU.mult, ALU.mult)
            ins.then_inc(gates_ready.sem, 1)
            dve.sem_inc(params_free, 1)

            def activate(slot, n, gated):
                dve.wait_ge(silu_ready.sem, silu_ready.by(layer, n))
                dst = act[:, slot]
                if gated:
                    tt(silu[:, slot], silu[:, slot], ps[:, 2:4, 0:T], ALU.mult).then_inc(act_gated.sem, 1)
                    dve.wait_ge(act_gated.sem, act_gated.by(layer, n))
                    ins = tt(dst, silu[:, slot], ps[:, 4, 0:T].unsqueeze(1).to_broadcast([P, 2, T]), ALU.mult)
                else:
                    tt(silu[:, slot], silu[:, slot], ps[:, 2:4, 0:T], ALU.mult).then_inc(act_gated.sem, 1)
                    dve.wait_ge(act_gated.sem, act_gated.by(layer, n))
                    ins = cp(dst, silu[:, slot])
                ins.then_inc(act_ready.sem, 1)

            def spread_gate(slot, e):
                ts(gd[:, slot, :], gT[:, :], cst[0:NE, bass.ds(K_ID + e, 1)] if not isinstance(e, int) else cst[0:NE, K_ID + e:K_ID + e + 1],
                   None, ALU.mult).then_inc(ge_ready.sem, 1)

            def add_down(n):
                dve.wait_ge(down_added.sem, down_added.by(layer, KD * n + 3))
                for c in range(KD):
                    dve.wait_ge(down_made.sem, down_made.by(layer, KD * n + c + 1))
                    tt(acc[:, c, :], acc[:, c, :], ps[:, 5 + c % 3, 0:T], ALU.add).then_inc(down_added.sem, 1)

            activate(1, 1, False)
            W(gates_turned)
            chain(cp(gT[:, :], ps[0:NE, 7, 0:T]))
            spread_gate(0, 0)
            dve.wait_ge(acc_zero.sem, acc_zero.by(layer, 1))
            held()
            with dve.Fori(0, NE, 2) as e0:
                for j in range(2):
                    activate(j, e0 + j + 2, True)
                    spread_gate(1 - j, e0 + j + 1)
                    add_down(e0 + j)
            add_down(NE)
            W(down_added, KD * (NE + 1) + 3)
            for c in range(KD):
                stt(xT[:, c, 0:NP_], acc[:, c, 0:NP_], modT[:, 40 + c, 0:1], xT[:, c, 0:NP_], ALU.mult, ALU.add)
            chain(tt(acc[:, :, NP_:T], acc[:, :, NP_:T], modT[:, 40:48, 1:NC], ALU.mult))
            tt(xT[:, :, NP_:T], xT[:, :, NP_:T], acc[:, :, NP_:T], ALU.add).then_inc(x_ready.sem, 1)
            chain.check()
        chain.leave()
        norm(lambda: dve.wait_ge(last["sumsq"], 1), 0, last["var"], lambda: dve.wait_ge(last["sd"], 1),
             finalg, None, last["h"])

    for cm in reversed(ctx_list):
        cm.__exit__(None, None, None)


SCALAR_LINKS, VECTOR_LINKS = 5, 131

OUTPUTS = [
    ("y_prompt", (1, NP_, D)), ("y_sample", (NS, 1, D)),
    ("k_prompt", (1, DEPTH, NP_, HEADS, 2 * HD)), ("v_prompt", (1, DEPTH, NP_, HEADS, VD)),
    ("pool_prompt", (1, DEPTH, PREV, POOL_W)),
    ("ssm_re_prompt", (1, DEPTH, SG, SN)), ("ssm_im_prompt", (1, DEPTH, SG, SN)),
    ("k_sample", (NS, DEPTH, 1, HEADS, 2 * HD)), ("v_sample", (NS, DEPTH, 1, HEADS, VD)),
    ("pool_sample", (NS, DEPTH, PREV, POOL_W)),
    ("ssm_re_sample", (NS, DEPTH, SG, SN)), ("ssm_im_sample", (NS, DEPTH, SG, SN)),
]


def kernel(**inputs):
    import concourse.bacc as bacc
    from concourse.bass_utils import run_bass_kernel_spmd

    nc = bacc.Bacc("TRN2", target_bir_lowering=False, num_devices=1)
    arrays, ins = {}, {}
    for name, x in [*inputs.items(), ("consts", shape_constants())]:
        x = np.ascontiguousarray(x)
        arrays[f"in_{name}"] = x
        ins[name] = nc.dram_tensor(f"in_{name}", x.shape, mybir.dt.from_np(x.dtype), kind="ExternalInput").ap()
    outs = {name: nc.dram_tensor(f"out_{name}", shape, F32, kind="ExternalOutput").ap() for name, shape in OUTPUTS}
    program(nc, ins, outs)
    r = run_bass_kernel_spmd(nc, [arrays], core_ids=[0])
    return tuple(r.results[0][f"out_{name}"] for name, _ in OUTPUTS)
```

```python
import math

import numpy as np

import concourse.bass as bass
from concourse import mybir

F32 = mybir.dt.float32
I32 = mybir.dt.int32
F32R = mybir.dt.float32r
ACT = mybir.ActivationFunctionType
ALU = mybir.AluOpType
AX = mybir.AxisListType

P = 128
D = 1024
KD = D // P
DEPTH = 2
NP_ = 256
NS = 8
T = NP_ + NS
NC = 1 + NS
EPS = 1e-6

POOL_W, HEADS, HD, VD = 256, 4, 64, 128
WINDOWS = (2, 4, 8, 16)
PREV = 15
IN_W = 2048
C_POOL, C_Q, C_K, C_V, C_U = 0, 2, 6, 10, 14
PROJ = IN_W // P

SG, SN, SCH = 16, 64, 16
SC = SG * SN // P
PAST, PAGE = 256, 128
PAGES = PAST // PAGE
ROWS = NS * HEADS * 2

NE, TOPK, NG, TOPG = 64, 8, 8, 4
PG = NE // NG
assert TOPK == 8 and PG == 8
SCALE_R = 2.5

SEG = 2048
ADA_SEGS, IN_SEGS, OUT_SEGS = 6 * D // 256, IN_W // 256, D // 256
WIDE_ADA, WIDE_IN = ADA_SEGS // 2, IN_SEGS // 2
WIDE_OUT = WIDE_ADA + WIDE_IN
WIDE_SHARED = WIDE_OUT + 1
WIDE_EXP = WIDE_SHARED + 1
WIDE_FILLS = WIDE_EXP + NE
NARROW_SHARED = OUT_SEGS - 1
ADA_FIRST = 4
NARROW_EXP = NARROW_SHARED + 1
NARROW_FILLS = NARROW_EXP + NE
assert WIDE_FILLS % 2 == 0 and NARROW_FILLS % 2 == 0 and WIDE_EXP % 2 == 0 and NARROW_EXP % 2 == 0

NEG = -1e30
ROUND = 12582912.0
TWO_PI_A = 6.28125
TWO_PI_B = 2 * math.pi - 6.28125

R_BADA, R_N1, R_N2, R_PS, R_SD, R_GB, R_SUB, R_AR, R_AI = 0, 48, 56, 64, 66, 68, 70, 71, 79
R_ALL = R_AI + SC

BUCKET_COLS = NP_ + P + 1
K_ID = 0
K_INV = K_ID + P
K_T = K_INV + 2 * NP_
K_HALF = K_T + NP_
K_LOW = K_HALF + 2
K_CMB = K_LOW + NG * NG
K_M0 = K_CMB + NS * HEADS
K_M1 = K_M0 + 1
K_AB = K_M1 + 1
K_BKT = K_AB + NS
K_LAM = K_BKT + PAST + 1
K_ONE = K_LAM + 2 * DEPTH
K_END = K_ONE + P


def shape_constants():
    c = np.zeros((P, K_END), np.float32)
    c[:, K_ID:K_ID + P] = np.eye(P)
    t = np.arange(NP_)
    for half in range(4):
        rows = slice(64 * (half % 2), 64 * (half % 2) + 64)
        cols = slice(K_INV + NP_ * (half // 2), K_INV + NP_ * (half // 2) + NP_)
        c[rows, cols] = 1.0 / np.minimum(WINDOWS[half], t + 1)
    c[:, K_T:K_T + NP_] = t
    for h in range(2):
        c[64 * h:64 * h + 64, K_HALF + h] = 1.0
    low = np.arange(NG)[None, :] < np.arange(NG)[:, None]
    c[:, K_LOW:K_LOW + NG * NG] = low.reshape(-1)
    row = np.arange(ROWS)
    c[row, K_CMB + row // 2] = 1.0
    c[row, K_M0] = row % 2 == 0
    c[row, K_M1] = row % 2 == 1
    c[row, K_AB + row // (2 * HEADS)] = 1.0
    n = np.arange(PAST + 1)
    large = 16 + (np.log(np.maximum(n, 1).astype(np.float32) / 16) / math.log(8.0) * 16).astype(np.int32)
    bucket = np.where(n < 16, n, np.minimum(large, 31))
    c[bucket, K_BKT + PAST - n] = 1.0
    for l in range(DEPTH):
        init = 0.8 - 0.6 * math.exp(-0.3 * l)
        c[:, K_LAM + 2 * l] = init
        c[:, K_LAM + 2 * l + 1] = 1.0 - init
    c[:, K_ONE:K_ONE + P] = 1.0
    return c


class Signal:

    def __init__(self, sem, per_layer):
        self.sem, self.per_layer = sem, per_layer

    def by(self, layer, k):
        return layer * self.per_layer + k


class Links:

    def __init__(self, eng, sem, per_layer):
        self.eng, self.sem, self.per_layer = eng, sem, per_layer
        self.before, self.made, self.layer = 0, 0, None

    def enter(self, layer):
        self.before, self.made, self.layer = self.made, 0, layer

    def check(self):
        assert self.made == self.per_layer, (self.made, self.per_layer)

    def leave(self):
        self.made, self.layer = self.before + DEPTH * self.per_layer, None

    def __call__(self, ins):
        self.wait(self.mark(ins))

    def mark(self, ins):
        self.made += 1
        ins.then_inc(self.sem, 1)
        return self.made

    def wait(self, link):
        at = link if self.layer is None else self.layer * self.per_layer + self.before + link
        self.eng.wait_ge(self.sem, at)


def program(nc, a, out):
    ctx_list = []

    def keep(cm):
        ctx_list.append(cm)
        return cm.__enter__()

    places = {}

    def sb(name, shape, dt=F32):
        places[name] = -(-nc.sbuf_base // 32) * 32
        return keep(nc.sbuf_tensor(name, shape, dt))

    def rounded(name, of, first, shape):
        return nc.alloc_sbuf_tensor_at(name, shape, F32R, offset=places[of] + 4 * first)

    def sem(name):
        return keep(nc.semaphore(name))

    def sig(name, per_layer):
        return Signal(sem(name), per_layer)

    cst = sb("cst", [P, K_END])
    xT = sb("xT", [P, KD, T])
    hT = sb("hT", [P, KD, T])
    projT = sb("projT", [P, PROJ, T])
    mixT = sb("mixT", [P, KD, T])
    wide = sb("wide", [P, 2, 2, SEG])
    narrow = sb("narrow", [P, 2, SEG])
    kbuf = sb("kbuf", [P, 2, PAGES, 512])
    vbuf = sb("vbuf", [P, 4, PAGES, 512])
    cosT = sb("cosT", [P, SC, NP_])
    sinT = sb("sinT", [P, SC, NP_])
    oT = sb("oT", [P, HEADS, T])
    rowsP = sb("rowsP", [P, 4, 512])
    biasT = sb("biasT", [P, HEADS, NP_])
    biasS = sb("biasS", [ROWS, PAST + 1])
    scratch = sb("scratch", [P, 4224])
    prow = sb("prow", [R_ALL, P])
    hrow = sb("hrow", [P, P])
    pT = sb("pT", [P, R_ALL])
    h0T = sb("h0T", [P, 2, NS, SC])
    dtall = sb("dtall", [P, SG])
    bst = sb("bst", [P, 2, SC, SCH])
    crow = sb("crow", [P, 2, 2, SN])
    bpad = sb("bpad", [P, 2, SC, 2, SCH])
    bbT = sb("bbT", [P, 2, 2, P])
    cT = sb("cT", [P, 2, 2, P])
    gluw = sb("gluw", [P, 2, 256])
    rw = sb("rw", [P, KD, NE])
    rbias = sb("rbias", [P, NE])
    poolw = sb("poolw", [P, 2, P])
    prevrow = sb("prevrow", [NS * PREV, POOL_W])
    ueS = sb("ueS", [P, 2, NS, PREV + 1])
    lamv = sb("lamv", [P, 4, HD])
    modT = sb("modT", [P, 48, NC])
    scA = sb("scA", [P, 2, KD, NC])
    condT = sb("condT", [P, KD, NC])
    finalg = sb("finalg", [P, KD])
    rowsS = sb("rowsS", [NS, 14 * P])
    poolrow = sb("poolrow", [PREV, POOL_W])
    w32 = sb("w32", [P, PAGES, NS, NS * HEADS])
    relb = sb("relb", [32, HEADS])
    relbs = sb("relbs", [32, NS, HEADS, 2])
    decS = sb("decS", [P, PAGES, ROWS])
    prodm = sb("prodm", [P, NS, HEADS, 2])
    qk = sb("qk", [P, NS, HEADS])
    comb = sb("comb", [ROWS, NS * HEADS])
    aps = sb("aps", [ROWS, NS])
    wself = sb("wself", [NS, NS * HEADS])
    sm = sb("sm", [P, 64])
    sp_ = sb("sp_", [P, 24, SC])
    i0 = sb("i0", [P, 2, SC, NS])
    i0t = sb("i0t", [P, 2, SC, NS])
    stF = sb("stF", [P, 2, SC])
    stS = sb("stS", [P, 2, NS, SC])
    strow = sb("strow", [P, 2, P])
    rstd = sb("rstd", [P, T])
    scr = sb("scr", [P, 3, NE])
    g1 = sb("g1", [P, 3, NG])
    rank = sb("rank", [P, 3, NG])
    t8 = sb("t8", [P, 3, 8])
    gsum = sb("gsum", [P, 3])
    tick_p = sb("tick_p", [1, 24])
    tick_v = sb("tick_v", [1, 8])
    ticks = [0, 0]
    ps = keep(nc.psum_tensor("ps", [P, 8, 512], F32))

    skew = nc.dram_tensor("skew", (HEADS * P * BUCKET_COLS,), F32, kind="Internal").ap()

    ident = cst[:, K_ID:K_ID + P]
    ones = cst[:, K_ONE:K_ONE + P]
    half = cst[:, K_HALF:K_HALF + 2]
    xrows = projT[:, :, :].rearrange("p a b -> p (a b)")[:, 0:4 * D].rearrange("p (a b) -> p a b", a=4)
    skews = scratch[:, 0:HEADS * BUCKET_COLS].rearrange("p (h i) -> p h i", h=HEADS)
    modrow = scratch[0:NC, 0:1024].rearrange("p (a b) -> p a b", a=2)
    modrow_late = kbuf[0:NC, 0, :, :]
    ang = scratch[:, 1024:1024 + 4 * 512].rearrange("p (a j t) -> p a j t", a=4, j=2)
    prod = scratch[:, 0:1024].rearrange("p (g n) -> p g n", g=PAGES)
    od = scratch[0:NS * HEADS, 1024:1536]
    sbuf_s = scratch[:, 0:1024].rearrange("p (n m k) -> p n m k", n=2, m=2)
    sbuf_p = scratch[:, 1024:2048].rearrange("p (n m k) -> p n m k", n=2, m=2)
    sbuf_w = scratch[:, 2048:2560].rearrange("p (n k) -> p n k", n=2)
    sbuf_w0 = scratch[:, 2560:2816]
    sbuf_wT = scratch[:, 2816:3840].rearrange("p (n k q) -> p n k q", n=2, k=2)
    vflat = vbuf[:, :, :, :].rearrange("p a g n -> p (a g n)")
    osq = vflat[:, 0:HEADS * T].rearrange("p (h t) -> p h t", h=HEADS)
    osd = vflat[:, HEADS * T:2 * HEADS * T].rearrange("p (h t) -> p h t", h=HEADS)
    rot = scratch[:, 0:3072].rearrange("p (a j t) -> p a j t", a=6, j=2)
    hs = scratch[:, 3072:3072 + 4 * T].rearrange("p (r j t) -> p r j t", r=2, j=2)
    yv = scratch[:, 0:2 * T].rearrange("p (a t) -> p a t", a=2)
    zv = scratch[:, 2 * T:4 * T].rearrange("p (a t) -> p a t", a=2)
    gv = scratch[:, 4 * T:6 * T].rearrange("p (a t) -> p a t", a=2)
    bb = scratch[:, 3072:3328].rearrange("p (r k c) -> p r k c", r=2, k=SC)
    crow2 = scratch[:, 3328:3840].rearrange("p (r t n) -> p r t n", r=2, t=2)
    pe64 = scratch[0:ROWS, 1536:1536 + PAST + 1]
    selb = oT[0:NS, :, :].rearrange("p a b -> p (a b)")[:, 0:NS * P].rearrange("p (b q) -> p b q", b=NS)
    relbw = mixT[0:32, :, :].rearrange("p a b -> p (a b)")[:, 0:HEADS * P].rearrange("p (h q) -> p h q", h=HEADS)
    hflat = hT[:, :, :].rearrange("p a b -> p (a b)")
    span = 2 * (PREV + NP_)
    ue, win_a, win_b = (hflat[:, n * span:(n + 1) * span].rearrange("p (c t) -> p c t", c=2) for n in range(3))
    pooled = mixT[:, 0:2, :]
    silu = scratch[:, 0:4 * T].rearrange("p (n f t) -> p n f t", n=2, f=2)
    act = scratch[:, 4 * T:8 * T].rearrange("p (n f t) -> p n f t", n=2, f=2)
    scT = scratch[0:NE, 8 * T:9 * T]
    r_wide = rounded("r_wide", "wide", 0, [P, 2, 2, SEG])
    r_narrow = rounded("r_narrow", "narrow", 0, [P, 2, SEG])
    r_wide_hi = [[rounded(f"r_wide_hi{n}{t}", of, first, [P, SEG])[:, :] for t, (of, first) in enumerate(pair)]
                 for n, pair in enumerate(((("vbuf", 0), ("vbuf", SEG)), (("kbuf", 0), ("sinT", 0))))]
    r_narrow_hi = [rounded("r_narrow_hi0", "rowsP", 0, [P, SEG])[:, :],
                   rounded("r_narrow_hi1", "projT", KD * T, [P, SEG])[:, :]]
    r_h = rounded("r_h", "hT", 0, [P, KD, T])
    r_h_hi = rounded("r_h_hi", "mixT", 0, [P, KD, T])
    r_act = rounded("r_act", "scratch", 4 * T, [P, 2, 2, T])
    r_act_hi = rounded("r_act_hi", "scratch", 9 * T, [P, 2, 2, T])
    r_gT = rounded("r_gT", "cosT", 0, [NE, 2, T])
    r_pick = rounded("r_pick", "cosT", 2 * T, [NE, 2, P])

    def plain(t):
        return t.bitcast(F32)

    acc = projT[:, 0:KD, :]
    cflat = cosT[:, :, :].rearrange("p a b -> p (a b)")
    biased = cflat[:, 800:992].rearrange("p (t e) -> p t e", t=3)
    masked = cflat[:, 992:1184].rearrange("p (t e) -> p t e", t=3)
    pairs = cflat[:, 1184:1376].rearrange("p (t g e) -> p t g e", t=3, g=NG)
    pairs2 = cflat[:, 1376:1568].rearrange("p (t g e) -> p t g e", t=3, g=NG)
    g8 = cflat[:, 1568:1760].rearrange("p (t g e) -> p t g e", t=3, g=NG)

    start_loaded = sem("start_loaded")
    pages_loaded = sem("pages_loaded")
    start_ready = sem("start_ready")
    start_zeroed = sem("start_zeroed")
    start_copied_v = sem("start_copied_v")
    start_copied_a = sem("start_copied_a")
    start_vector = sem("start_vector")
    start_silu = sem("start_silu")
    skew_moved = sem("skew_moved")
    wide_free, wide_loaded = sem("wide_free"), [sem("wide_loaded0"), sem("wide_loaded1")]
    narrow_free, narrow_loaded = sem("narrow_free"), [sem("narrow_loaded0"), sem("narrow_loaded1")]
    params_free = sem("params_free")
    N_PARAM = 33
    params_loaded = sig("params_loaded", 16 * N_PARAM)
    rows_turned = sig("rows_turned", 1)
    rows_copied = sig("rows_copied", 1)
    crow_ready = sig("crow_ready", 1)
    c_turned = sig("c_turned", 1)
    bpad_ready = sig("bpad_ready", 1)
    b_turned = sig("b_turned", 1)
    cb_copied = sig("cb_copied", 2)
    dt_ready = sig("dt_ready", 1)
    mag_in = sig("mag_in", 1)
    mag_ready = sig("mag_ready", 1)
    angle_ready = sig("angle_ready", 1 + SC // 2)
    sines_ready = sig("sines_ready", 1 + SC // 2)
    lam_sums = sig("lam_sums", 1)
    lam_exp = sig("lam_exp", 1)
    ada_made = sig("ada_made", 12)
    ada_copied = sig("ada_copied", 12)
    ada_turned = sig("ada_turned", 12)
    ada_late = sig("ada_late", WIDE_ADA - ADA_FIRST)
    mod_ready = sig("mod_ready", 2)
    squares = sig("squares", 2)
    sumsq = sig("sumsq", 2)
    var_ready = sig("var_ready", 2)
    sd_ready = sig("sd_ready", 2)
    h_ready = sig("h_ready", 4)
    proj_made = sig("proj_made", PROJ)
    proj_copied_a = sig("proj_copied_a", PROJ // 2)
    proj_copied_v = sig("proj_copied_v", PROJ // 2)
    srows_made = sig("srows_made", 1)
    srows_copied = sig("srows_copied", 1)
    prows_made = sig("prows_made", 1)
    prows_copied = sig("prows_copied", 1)
    k_loaded = [sig(f"k_loaded{n}", 16 * PAGES * NS // 2) for n in range(2)]
    v_loaded = [sig(f"v_loaded{n}", 16 * PAGES * NS // 4) for n in range(4)]
    q_spread = sig("q_spread", NS)
    dec_products = sig("dec_products", NS)
    dec_scored = sig("dec_scored", 1)
    dec_turned = sig("dec_turned", 1)
    dec_max = sig("dec_max", 1)
    dec_exp = sig("dec_exp", 1)
    comb_ready = sig("comb_ready", 1)
    dec_weights = sig("dec_weights", 1)
    w32_ready = sig("w32_ready", 1)
    dec_pv = sig("dec_pv", NS)
    dec_o_copied = sig("dec_o_copied", 1)
    dec_o_turned = sig("dec_o_turned", 1)
    scored = sig("scored", 2 * HEADS)
    biased_ready = sig("biased_ready", 2 * HEADS)
    negmax = sig("negmax", 2 * HEADS)
    probs = sig("probs", 2 * HEADS)
    w_ready = sig("w_ready", 2 * HEADS)
    w_turned = sig("w_turned", 2 * HEADS)
    w_copied = sig("w_copied", 2 * HEADS)
    pv_made = sig("pv_made", HEADS)
    pv_copied = sig("pv_copied", HEADS)
    o_ready = sig("o_ready", 1)
    o_squared = sig("o_squared", 1)
    o_sums = sig("o_sums", 1)
    o_var = sig("o_var", 1)
    o_sd = sig("o_sd", 1)
    o_normed = sig("o_normed", 1)
    attn_mixed = sig("attn_mixed", 1)
    pool_sample = sig("pool_sample", 1)
    pool_prompt = sig("pool_prompt", 1)
    pool_made = sig("pool_made", 2)
    pool_mixed = sig("pool_mixed", 2)
    bu_made = sig("bu_made", SC // 2)
    bu_used = sig("bu_used", SC // 2)
    hs_ready = sig("hs_ready", SC // 2)
    y_made = sig("y_made", SC // 2)
    y_ready = sig("y_ready", 1)
    gelu_ready = sig("gelu_ready", 1)
    glu_made = sig("glu_made", 1)
    glu_gate = sig("glu_gate", 1)
    ssm_mixed = sig("ssm_mixed", 1)
    st_ready = sig("st_ready", 1)
    st_turned = sig("st_turned", 1)
    st_copied = sig("st_copied", 1)
    out_made = sig("out_made", KD)
    out_added = sig("out_added", KD)
    logits = sig("logits", 1)
    scores_sig = sig("scores_sig", 1)
    scores_turned = sig("scores_turned", 1)
    gates_ready = sig("gates_ready", 1)
    gates_turned = sig("gates_turned", 1)
    acc_zero = sig("acc_zero", 1)
    ge_ready = sig("ge_ready", NE + 2)
    act_step = sig("act_step", 3 * (NE + 1))
    gate_made = sig("gate_made", NE + 1)
    gu_made = sig("gu_made", NE + 1)
    high_h, low_h = sig("high_h", 1), sig("low_h", 1)
    high_wide, low_wide = sig("high_wide", 2 * (NE + 1)), sig("low_wide", 2 * (NE + 1))
    high_narrow, low_narrow = sig("high_narrow", NE + 1), sig("low_narrow", NE + 1)
    silu_ready = sig("silu_ready", NE + 1)
    act_ready = sig("act_ready", NE + 1)
    down_made = sig("down_made", KD * (NE + 1))
    down_added = sig("down_added", KD * (NE + 1))
    x_ready = sig("x_ready", 1)
    cache_stored = sem("cache_stored")
    stores = sem("stores")
    y_stored = sem("y_stored")
    N_STORE = 4 + 1 + 3 + NS + 2 + 2 * NS
    last = {k: sem("last_" + k) for k in ("squares", "sumsq", "var", "sd", "h", "turned", "copied")}
    vlink, alink, plink = sem("vector_link"), sem("scalar_link"), sem("pool_link")
    layer_stores = Signal(stores, 16 * N_STORE)

    def unit_wide(layer, e0, j):
        k = WIDE_SHARED + 1 + j
        return wide_loaded[k % 2], 32 * (layer * (WIDE_FILLS // 2) + k // 2 + 1) + 16 * e0

    def unit_narrow(layer, e0, j):
        k = NARROW_SHARED + 1 + j
        return narrow_loaded[k % 2], 16 * (layer * (NARROW_FILLS // 2) + k // 2 + 1) + 8 * e0

    block = keep(nc.Block())

    def wide_at(layer, f):
        return wide_loaded[f % 2], 32 * (layer * (WIDE_FILLS // 2) + f // 2 + 1)

    def narrow_at(layer, f):
        return narrow_loaded[f % 2], 16 * (layer * (NARROW_FILLS // 2) + f // 2 + 1)

    @block.sync
    def _(sp):
        def columns(w, s):
            return w[:, 256 * s:256 * s + 256].rearrange("(k p) n -> p k n", p=P)

        def seg(t):
            return t.rearrange("p (k n) -> p k n", k=KD)

        def load(sem_, dst, src):
            sp.dma_start(dst, src, allow_slow_non_contiguous=True).then_inc(sem_, 16)

        def load_parameters(layer):
            sp.wait_ge(start_zeroed, 1)
            sp.wait_ge(params_free, layer + 1)
            n0 = [0]

            def par(dst, src):
                n0[0] += 1
                load(params_loaded.sem, dst, src)

            def rows(v):
                return v.rearrange("(k p) -> k p", p=P)

            par(prow[R_BADA:R_BADA + 48, :], rows(a["b_ada"][layer]))
            par(prow[R_N1:R_N1 + 8, :], rows(a["norm1_g"][layer]))
            par(prow[R_N2:R_N2 + 8, :], rows(a["norm2_g"][layer]))
            par(prow[R_PS:R_PS + 2, :], rows(a["pool_scale"][layer]))
            par(prow[R_SD:R_SD + 2, :], rows(a["ssm_d"][layer]))
            par(prow[R_GB:R_GB + 2, :], rows(a["glu_b"][layer]))
            par(prow[R_SUB:R_SUB + 1, :], rows(a["subln_g"][layer]))
            par(prow[R_AR:R_AR + 8, :], a["ssm_a_re"][layer].rearrange("(k g) n -> k (g n)", g=2))
            par(prow[R_AI:R_AI + 8, :], a["ssm_a_im"][layer].rearrange("(k g) n -> k (g n)", g=2))
            par(dtall[:, :], a["ssm_log_dt"][layer].partition_broadcast(P))
            for r, name in enumerate(("state_ssm_re", "state_ssm_im")):
                v = a[name].rearrange("b l (k g) n -> l b k (g n)", g=2)[layer]
                for q in range(2):
                    par(hrow[64 * r + 32 * q:64 * r + 32 * q + 32, :], v[4 * q:4 * q + 4])
            for r, name in enumerate(("ssm_b_re", "ssm_b_im")):
                par(bst[:, r], a[name][layer].rearrange("(k g) n c -> (g n) k c", g=2))
            for r, name in enumerate(("ssm_c_re", "ssm_c_im")):
                par(crow[:, r], a[name][layer].rearrange("(t g) c n -> (g c) t n", t=2))
            par(gluw[:, :, :], a["glu_w"][layer].rearrange("(k p) n -> p k n", p=P))
            par(rw[:, :, :], a["router_w"][layer].rearrange("(k p) n -> p k n", p=P))
            par(rbias[:, :], a["router_bias"][layer].partition_broadcast(P))
            for n, name in enumerate(("lam_q1", "lam_k1", "lam_q2", "lam_k2")):
                par(lamv[:, n, :], a[name][layer].partition_broadcast(P))
            for g in range(4):
                r0 = 64 * (g % 2)
                par(poolw[r0:r0 + 64, g // 2, r0:r0 + 64], a["pool_w"][layer, g])
            for b in range(NS):
                if b % 2 == 0:
                    par(prevrow[PREV * b:PREV * b + 2 * PREV, :], a["state_pool"].rearrange("b l t c -> l b t c")[layer, b:b + 2])
            assert n0[0] == N_PARAM, n0

        load(start_loaded, cst[:, :], a["consts"])
        for t in range(2):
            load(start_loaded, xrows[:, t, :], a["x_prompt"][0, P * t:P * t + P, :])
        load(start_loaded, xrows[0:NS, 2, :], a["x_sample"][:, 0, :])
        load(start_loaded, xrows[0:1, 3, :], a["c_prompt"])
        load(start_loaded, xrows[1:NC, 3, :], a["c_sample"])
        load(start_loaded, relb[:, :], a["rel_bias"])
        load(start_loaded, hrow[0:KD, :], a["final_g"].rearrange("(k p) -> k p", p=P))
        sp.sem_inc(wide_free, 2)
        sp.sem_inc(narrow_free, 2)
        with sp.Fori(0, DEPTH) as layer:
            ada, win, wout = a["w_ada"][layer], a["w_in"][layer], a["w_out"][layer]
            for f in range(WIDE_OUT):
                if f < ADA_FIRST:
                    w, s = ada, 2 * f
                elif f < ADA_FIRST + WIDE_IN:
                    w, s = win, 2 * (f - ADA_FIRST)
                else:
                    w, s = ada, 2 * (f - WIDE_IN)
                if f == 2:
                    load_parameters(layer)
                sp.wait_ge(wide_free, layer * WIDE_FILLS + f + 1)
                for j in range(2):
                    sp.dma_start(seg(wide[:, f % 2, j]), columns(w, s + j)).then_inc(wide_loaded[f % 2], 16)
            sp.wait_ge(wide_free, layer * WIDE_FILLS + WIDE_OUT + 1)
            for j in range(2):
                sp.dma_start(seg(wide[:, WIDE_OUT % 2, 0])[:, 4 * j:4 * j + 4],
                             columns(wout, 0)[:, 4 * j:4 * j + 4]).then_inc(wide_loaded[WIDE_OUT % 2], 16)
            for f in range(NARROW_SHARED):
                sp.wait_ge(narrow_free, layer * NARROW_FILLS + f + 1)
                sp.dma_start(seg(narrow[:, f % 2]), columns(wout, f + 1)).then_inc(narrow_loaded[f % 2], 16)

            def gate_up(g, u, f, slot):
                sp.wait_ge(wide_free, layer * WIDE_FILLS + f + 1)
                for j, w in enumerate((g, u)):
                    sp.dma_start(seg(wide[:, slot, j]), w.rearrange("(k p) n -> p k n", p=P)).then_inc(wide_loaded[slot], 16)

            def down(d, f, slot):
                sp.wait_ge(narrow_free, layer * NARROW_FILLS + f + 1)
                sp.dma_start(narrow[:, slot].rearrange("p (k n) -> p k n", k=2),
                             d.rearrange("(k p) n -> p k n", p=P)).then_inc(narrow_loaded[slot], 16)

            wg, wu, wd = (a[n].rearrange("l (e j) r c -> (l e) j r c", j=2) for n in ("exp_w_gate", "exp_w_up", "exp_w_down"))
            first = layer * (NE // 2)
            gate_up(a["shared_w_gate"][layer], a["shared_w_up"][layer], WIDE_SHARED, 1)
            gate_up(wg[first, 0], wu[first, 0], WIDE_EXP, 0)
            down(a["shared_w_down"][layer], NARROW_SHARED, 1)
            gate_up(wg[first, 1], wu[first, 1], WIDE_EXP + 1, 1)
            with sp.Fori(0, NE // 2 - 1) as pair:
                e, e0 = first + pair, 2 * pair
                down(wd[e, 0], NARROW_EXP + e0, 0)
                gate_up(wg[e + 1, 0], wu[e + 1, 0], WIDE_EXP + e0 + 2, 0)
                down(wd[e, 1], NARROW_EXP + e0 + 1, 1)
                gate_up(wg[e + 1, 1], wu[e + 1, 1], WIDE_EXP + e0 + 3, 1)
            end = first + NE // 2 - 1
            for j in range(2):
                down(wd[end, j], NARROW_EXP + NE - 2 + j, j)
        yrows = projT[:, :, :].rearrange("p a b -> p (a b)")[:, 0:3 * D].rearrange("p (a b) -> p a b", a=3)
        for t in range(3):
            sp.wait_ge(last["copied"], 2 * t + 2)
            dst, n = (out["y_prompt"][0, P * t:P * t + P, :], P) if t < 2 else (out["y_sample"][:, 0, :], NS)
            sp.dma_start(dst, yrows[0:n, t, :]).then_inc(y_stored, 16)
        sp.wait_ge(y_stored, 48)

    @block.gpsimd
    def _(pool):
        gp = nc.gpsimd

        def load(sem_, dst, src):
            pool.dma_start(dst, src, allow_slow_non_contiguous=True).then_inc(sem_, 16)

        chain = Links(pool, plink, 9)

        def held():
            ticks[0] += 1
            gp.tensor_tensor(tick_p[:, ticks[0] - 1:ticks[0]], cst[0:1, K_ONE:K_ONE + 1], cst[0:1, K_ONE:K_ONE + 1], ALU.add)

        gp.memset(poolw[:, :, :], 0.0).then_inc(start_zeroed, 1)
        gp.memset(w32[:, :, :, :], 0.0)
        gp.memset(skews[:, :, PAST + 1:], NEG)
        chain(gp.memset(scr[:, :, :], 0.0))
        pool.wait_ge(start_copied_a, 4)
        load(skew_moved, skew.rearrange("(h p i) -> p h i", h=HEADS, p=P), skews)
        pool.wait_ge(skew_moved, 16)
        for h in range(HEADS):
            src = bass.AP(skew.tensor, h * P * BUCKET_COLS + P, [[BUCKET_COLS - 1, P], [1, NP_]])
            load(skew_moved, biasT[:, h, :], src)

        kc, vc = a["cache_k"], a["cache_v"]
        pt = sb("pt", [1, NS * PAGES], I32)
        load(pages_loaded, pt[:, :], a["page_table"].rearrange("b n -> (b n)")[None, :])
        pool.wait_ge(start_loaded, 16 * 8)
        pool.wait_ge(pages_loaded, 16)
        pool.wait_ge(start_vector, 2)
        pages = [pool.value_load(pt[0:1, n:n + 1], min_val=0, max_val=kc.shape[0] - 1) for n in range(NS * PAGES)]
        kcf = kc.rearrange("n l t h d -> (n l) t (h d)")
        vcf = vc.rearrange("n l t h d -> (n l) t (h d)")
        pool.sem_inc(cache_stored, 1)
        with pool.Fori(0, DEPTH) as layer:
            chain.enter(layer)
            def load_k(b):
                for g in range(PAGES):
                    load(k_loaded[b % 2].sem, kbuf[:, b % 2, g, :], kcf[pages[b * PAGES + g] * DEPTH + layer])

            def load_v(b):
                for g in range(PAGES):
                    load(v_loaded[b % 4].sem, vbuf[:, b % 4, g, :], vcf[pages[b * PAGES + g] * DEPTH + layer])

            pool.wait_ge(x_ready.sem, x_ready.by(layer, 1))
            held()
            for b in range(2):
                load_k(b)
            for b in range(4):
                load_v(b)
            for b in range(2, NS):
                pool.wait_ge(dec_products.sem, dec_products.by(layer, b - 1))
                held()
                load_k(b)

            pool.wait_ge(proj_made.sem, proj_made.by(layer, PROJ))
            pool.wait_ge(proj_copied_a.sem, proj_copied_a.by(layer, 1))
            pool.wait_ge(proj_copied_v.sem, proj_copied_v.by(layer, 1))
            held()
            gp.memset(ue[:, :, 0:PREV], 0.0)
            chain(gp.tensor_copy(ue[:, :, PREV:], projT[:, C_POOL:C_POOL + 2, 0:NP_]))
            inv = cst[:, K_INV:K_INV + 2 * NP_].rearrange("p (c t) -> p c t", c=2)
            source = ue
            L = PREV + NP_
            for n, w in enumerate(WINDOWS):
                dest = (win_a, win_b)[n % 2]
                lo, s = w - 1, w // 2
                chain(gp.tensor_tensor(dest[:, :, lo:L], source[:, :, lo:L], source[:, :, lo - s:L - s], ALU.add))
                rows_, c = slice(64 * (n % 2), 64 * (n % 2) + 64), n // 2
                chain(gp.tensor_tensor(pooled[rows_, c, 0:NP_], dest[rows_, c, PREV:], inv[rows_, c, :], ALU.mult))
                source = dest
            gp.tensor_tensor(pooled[:, :, 0:NP_], pooled[:, :, 0:NP_], ue[:, :, PREV:], ALU.subtract)\
                .then_inc(pool_prompt.sem, 1)

            for b in range(4, NS):
                pool.wait_ge(dec_pv.sem, dec_pv.by(layer, b - 3))
                held()
                load_v(b)

            def store(dst, src):
                st[0] += 1
                pool.dma_start(dst, src, allow_slow_non_contiguous=True).then_inc(stores, 16)

            st = [0]
            pool.wait_ge(prows_copied.sem, prows_copied.by(layer, 1))
            held()
            for n, name in enumerate(("k_prompt", "v_prompt")):
                o = out[name].rearrange("b l s h d -> b l s (h d)")
                for t in range(2):
                    store(o[0, layer, P * t:P * t + P, :], rowsP[:, 2 * n + t, :])
            store(out["pool_prompt"][0, layer], poolrow[:, :])
            pool.wait_ge(srows_copied.sem, srows_copied.by(layer, 1))
            held()
            store(out["k_sample"].rearrange("b l s h d -> l b (s h d)")[layer], rowsS[:, 512:1024])
            store(out["v_sample"].rearrange("b l s h d -> l b (s h d)")[layer], rowsS[:, 1024:1536])
            ps_o = out["pool_sample"].rearrange("b l t c -> l b t c")
            store(ps_o[layer, :, PREV - 1, :], rowsS[:, 1536:1792])
            pool.wait_ge(params_loaded.sem, params_loaded.by(layer, 16 * N_PARAM))
            held()
            for b in range(NS):
                store(ps_o[layer, b, 0:PREV - 1, :], prevrow[PREV * b + 1:PREV * b + PREV, :])

            pool.wait_ge(st_copied.sem, st_copied.by(layer, 1))
            held()
            for r, name in enumerate(("ssm_re_prompt", "ssm_im_prompt")):
                store(out[name][0, layer].rearrange("(k g) n -> k (g n)", g=2), strow[SC * r:SC * r + SC, 0, :])
            for r, name in enumerate(("ssm_re_sample", "ssm_im_sample")):
                o = out[name].rearrange("b l (k g) n -> l b k (g n)", g=2)[layer]
                for b in range(NS):
                    store(o[b], strow[64 * r + SC * b:64 * r + SC * b + SC, 1, :])
            pool.wait_ge(out_made.sem, out_made.by(layer, KD))
            pool.wait_ge(ssm_mixed.sem, ssm_mixed.by(layer, 1))
            held()
            gp.memset(acc, 0.0).then_inc(acc_zero.sem, 1)
            pool.wait_ge(stores, layer_stores.by(layer, 16 * st[0]))
            pool.sem_inc(cache_stored, 1)
            assert chain.made == chain.per_layer and 16 * st[0] == layer_stores.per_layer, (chain.made, st)
        pool.wait_ge(stores, DEPTH * layer_stores.per_layer)

    @block.tensor
    def _(pe):
        mm = nc.tensor.matmul

        def turn(dst, src, n):
            return nc.tensor.transpose(dst, src, ident[0:n, 0:n])

        def times_one(dst, src, n):
            return mm(dst, src, ident[0:n, 0:n], start=True, stop=True)

        pe.wait_ge(start_loaded, 16 * 8)
        for k in range(KD):
            if k >= 4:
                pe.wait_ge(start_copied_v, k - 3)
            for t in range(3):
                n = P if t < 2 else NS
                ins = turn(ps[:, k % 4, P * t:P * t + n], xrows[0:n, t, P * k:P * k + P], n)
            ins.then_inc(start_ready, 1)
        pe.wait_ge(start_vector, 1)
        for h in range(HEADS):
            mm(ps[:, 4 + h, 0:PAST + 1], relbw[:, h, :], cst[0:32, K_BKT:K_BKT + PAST + 1],
               start=True, stop=True).then_inc(start_ready, 1)
        pe.wait_ge(start_copied_v, 8)
        pe.wait_ge(start_silu, 1)
        for k in range(KD):
            turn(ps[:, 0, NC * k:NC * k + NC], xrows[0:NC, 3, P * k:P * k + P], NC)
        turn(ps[:, 1, 0:KD], hrow[0:KD, :], KD)
        mm(ps[0:ROWS, 2, 0:PAST + 1], relbs[:, :, :, :].rearrange("p a b c -> p (a b c)"),
           cst[0:32, K_BKT:K_BKT + PAST + 1], start=True, stop=True).then_inc(start_ready, 1)

        def sum_squares(bank, done):
            for k in range(KD):
                ins = mm(ps[:, bank, 0:T], ones, hT[:, k, :], start=k == 0, stop=k == KD - 1)
            ins.then_inc(done, 1)

        pe.wait_ge(start_vector, 2)
        with pe.Fori(0, DEPTH) as layer:
            def W(s, k=1):
                pe.wait_ge(s.sem, s.by(layer, k))

            W(x_ready)
            def ada_half(q, j, bank):
                f = q if q < ADA_FIRST else q + WIDE_IN
                if j == 0:
                    pe.wait_ge(*wide_at(layer, f))
                seg = wide[:, f % 2, j].rearrange("p (k n) -> p k n", k=KD)
                for k in range(KD):
                    ins = mm(ps[0:NC, bank, 256 * j:256 * j + 256], condT[:, k, :], seg[:, k, :],
                             start=k == 0, stop=k == KD - 1, skip_group_check=True)
                    if q not in (0, ADA_FIRST) and j + k == 0:
                        ins.then_inc(wide_free, 1)
                if j == 1:
                    ins.then_inc(ada_made.sem, 1)

            def ada_turn(q, bank, first):
                W(ada_copied, q + 1)
                rows_ = (modrow if q < ADA_FIRST else modrow_late)[:, q % 2, :]
                for j in range(4):
                    ins = times_one(ps[:, bank, first + NC * j:first + NC * j + NC], rows_[:, P * j:P * j + P], NC)
                    if q in (ADA_FIRST - 1, WIDE_ADA - 1) and j == 0:
                        ins.then_inc(wide_free, 1)
                ins.then_inc(ada_turned.sem, 1)

            for q in range(ADA_FIRST):
                if q >= 2:
                    W(ada_copied, q - 1)
                for j in range(2):
                    ada_half(q, j, q % 2)
                if q >= 1:
                    ada_turn(q - 1, 2, 4 * NC * (q - 1))
                if q == 1:
                    W(params_loaded, 16 * N_PARAM)
                    turn(ps[:, 4, 0:R_ALL], prow[:, :], R_ALL)
                    turn(ps[:, 4, P:2 * P], hrow[:, :], P)
                    for c in range(2):
                        ins = turn(ps[:, 5, P * c:P * c + NS * PREV], prevrow[:, P * c:P * c + P], NS * PREV)
                    ins.then_inc(rows_turned.sem, 1)
            ada_turn(ADA_FIRST - 1, 2, 4 * NC * (ADA_FIRST - 1))

            W(squares, 1)
            sum_squares(3, sumsq.sem)

            for c in range(PROJ):
                s, f = c // 2, ADA_FIRST + c // 4
                if c % 4 == 0:
                    pe.wait_ge(*wide_at(layer, f))
                if c >= 4:
                    W((proj_copied_a, proj_copied_v)[c % 2], (c - 4) // 2 + 1)
                w = wide[:, f % 2, s % 2].rearrange("p (k n) -> p k n", k=KD)
                for k in range(KD):
                    if c == 0 and k % (KD // 2) == 0:
                        W(h_ready, 1 + k // (KD // 2))
                    ins = mm(ps[:, c % 4, 0:T], w[:, k, P * (c % 2):P * (c % 2) + P], hT[:, k, :],
                             start=k == 0, stop=k == KD - 1)
                    if c >= 4 and c % 4 == 0 and k == 0:
                        ins.then_inc(wide_free, 1)
                ins.then_inc(proj_made.sem, 1)
                if c == PROJ - 5:
                    W(crow_ready)
                    for r in range(2):
                        for t in range(2):
                            ins = turn(ps[:, 6, P * (2 * r + t):P * (2 * r + t) + P], crow2[:, r, t, :], P)
                    ins.then_inc(c_turned.sem, 1)
                    W(bpad_ready)
                    for r in range(2):
                        for t in range(2):
                            ins = turn(ps[:, 7, P * (2 * r + t):P * (2 * r + t) + P],
                                       bpad[:, r, 4 * t:4 * t + 4].rearrange("p k h c -> p (k h c)"), P)
                    ins.then_inc(b_turned.sem, 1)

            W(proj_copied_a, PROJ // 2)
            W(proj_copied_v, PROJ // 2)
            W(cb_copied, 2)
            for n, c in enumerate([*range(C_Q, C_Q + 12), 0, 1]):
                ins = turn(ps[0:NS, 4 + n // 4, P * (n % 4):P * (n % 4) + P], projT[:, c, NP_:T], P)
                if n == 0:
                    ins.then_inc(wide_free, 1)
            ins.then_inc(srows_made.sem, 1)
            for n, c0 in enumerate((C_K, C_V)):
                for t in range(2):
                    for h in range(HEADS):
                        turn(ps[:, 2 * n + t, P * h:P * h + P], projT[:, c0 + h, P * t:P * t + P], P)
            W(srows_copied)
            for c in range(2):
                ins = turn(ps[0:PREV, 7, 256 + P * c:256 + P * c + P], projT[:, c, NP_ - PREV:NP_], P)
            ins.then_inc(prows_made.sem, 1)

            for b in range(NS):
                if b >= 2:
                    W(dec_products, b - 1)
                mm(ps[:, 4 + b % 2, :], selb[:, b, :], rowsS[:, 0:512], start=True, stop=True)\
                    .then_inc(q_spread.sem, 1)
            W(prows_copied)
            ada_half(ADA_FIRST, 0, 0)
            pe.wait_ge(dec_scored.sem, dec_scored.by(layer, 1))
            for g in range(PAGES):
                times_one(ps[0:ROWS, 6, P * g:P * g + P], decS[:, g, :], P)
            mm(ps[0:ROWS, 6, PAST:PAST + 1], prodm[:, :, :, :].rearrange("p a b c -> p (a b c)"), ones[:, 0:1],
               start=True, stop=True).then_inc(dec_turned.sem, 1)
            ada_half(ADA_FIRST, 1, 0)
            W(comb_ready)
            for g in range(PAGES):
                mm(ps[:, 7, 32 * g:32 * g + 32], pe64[:, P * g:P * g + P], comb[:, :], start=True, stop=True)
            mm(ps[0:NS, 7, 64:96], aps[:, :], comb[:, :], start=True, stop=True).then_inc(dec_weights.sem, 1)
            W(w32_ready)
            W(dec_products, NS)
            for b in range(NS):
                pe.wait_ge(v_loaded[b % 4].sem, v_loaded[b % 4].by(layer, 32 * (b // 4 + 1)))
                for g in range(PAGES):
                    ins = mm(ps[0:32, 5, :], w32[:, g, b, :], vbuf[:, b % 4, g, :], start=b + g == 0, stop=False)
                if b == 3:
                    ins.then_inc(dec_pv.sem, 1)
                    for j in range(2):
                        ada_half(ADA_FIRST + 1, j, 1)
                    ada_turn(ADA_FIRST, 2, 0)
                    continue
                if b == NS - 1:
                    ins = mm(ps[0:32, 5, :], wself[:, :], rowsS[:, 1024:1536], start=False, stop=True)
                ins.then_inc(dec_pv.sem, 1)
            ada_turn(ADA_FIRST + 1, 3, 0)
            pe.wait_ge(dec_o_copied.sem, dec_o_copied.by(layer, 1))
            for h in range(HEADS):
                ins = times_one(ps[:, 5, 32 * h:32 * h + 32], od[:, P * h:P * h + P], 32)
            ins.then_inc(dec_o_turned.sem, 1)

            def scores(n):
                h, i = n // 2, n % 2
                keys = P * (i + 1)
                if n >= 2:
                    W(biased_ready, n - 1)
                for m in range(2):
                    rows_ = slice(HD * m, HD * m + HD)
                    ins = mm(ps[:, 2 * (n % 2) + m, 0:keys], projT[rows_, C_Q + h, P * i:P * i + P],
                             projT[rows_, C_K + h, 0:keys], start=True, stop=True, skip_group_check=True)
                ins.then_inc(scored.sem, 1)

            W(ada_late, 2)
            scores(0)
            W(o_ready)
            for n in range(2 * HEADS):
                h, i = n // 2, n % 2
                q = ADA_FIRST + 2 + h
                if n + 1 < 2 * HEADS:
                    scores(n + 1)
                if i == 0 and h >= 1:
                    W(ada_copied, q)
                ada_half(q, i, 5)
                if i == 0 and h >= 1:
                    W(pv_copied, h)
                    ada_turn(q - 1, 4, 256)
                W(w_ready, n + 1)
                if n >= 2:
                    W(w_copied, n - 1)
                for t in range(i + 1):
                    ins = turn(ps[:, 6 + n % 2, P * t:P * t + P], sbuf_w[:, n % 2, P * t:P * t + P], P)
                ins.then_inc(w_turned.sem, 1)
                if i == 1:
                    W(w_copied, n + 1)
                    if h >= 1:
                        W(ada_late, 2 + h)
                    mm(ps[:, 4, 0:NP_], rowsP[:, 2, P * h:P * h + P], sbuf_wT[:, h % 2, 0, :],
                       start=True, stop=False)
                    mm(ps[:, 4, P:NP_], rowsP[:, 3, P * h:P * h + P], sbuf_wT[:, h % 2, 1, P:NP_],
                       start=False, stop=True).then_inc(pv_made.sem, 1)
            def drive(p):
                if p >= 1:
                    W(bu_used, p)
                for r in range(2):
                    for j in range(2):
                        c = 2 * p + j
                        rows_ = slice(32 * (c % 4), 32 * (c % 4) + 32)
                        ins = mm(ps[:, 2 * r + j, 0:T], bbT[rows_, r, c // 4, :], projT[rows_, C_U + c // 4, :],
                                 start=True, stop=True, tile_position=(32 * (c % 4), 0))
                ins.then_inc(bu_made.sem, 1)

            drive(0)
            W(pv_copied, HEADS)
            ada_turn(ADA_FIRST + 1 + HEADS, 4, 256)
            W(ada_late, 2 + HEADS)
            W(o_squared)
            W(w_copied, 2 * HEADS)
            for h in range(HEADS):
                ins = mm(ps[:, 4 + h, 0:T], ones, osq[:, h, :], start=True, stop=True)
            ins.then_inc(o_sums.sem, 1)
            for p in range(SC // 2):
                if p + 1 < SC // 2:
                    drive(p + 1)
                if p >= 2:
                    ada_turn(WIDE_ADA - 4 + p, 4 + p, 0)
                W(hs_ready, p + 1)
                if p == 0:
                    W(pool_prompt)
                    W(pool_sample)
                    W(o_var)
                    for c in range(2):
                        mm(ps[:, 6 + c, 0:T], poolw[:, c, :], pooled[:, c, :], start=True, stop=True)\
                            .then_inc(pool_made.sem, 1)
                for j in range(2):
                    c = 2 * p + j
                    cols = slice(32 * (c % 4), 32 * (c % 4) + 32)
                    for r in range(2):
                        ins = mm(ps[cols, 4 + c // 4, 0:T], cT[:, r, c // 4, cols], hs[:, r, j, :],
                                 start=r == 0, stop=r == 1, skip_group_check=True,
                                 tile_position=(0, 32 * (c % 4)))
                ins.then_inc(y_made.sem, 1)
                if p == 0:
                    W(pool_mixed, 2)
                    ada_half(WIDE_ADA - 2, 0, 6)
                elif p == 1:
                    ada_half(WIDE_ADA - 2, 1, 6)
                    ada_half(WIDE_ADA - 1, 0, 7)
                elif p == 2:
                    ada_half(WIDE_ADA - 1, 1, 7)
            W(st_ready)
            turn(ps[0:2 * SC, 0, 0:P], stF[:, :, :].rearrange("p a b -> p (a b)"), P)
            turn(ps[:, 1, 0:P], stS[:, :, :, :].rearrange("p a b c -> p (a b c)"), P).then_inc(st_turned.sem, 1)
            def out_part(c, ks):
                s = c // 2
                w = (wide[:, WIDE_OUT % 2, 0] if s == 0 else narrow[:, (s - 1) % 2]).rearrange("p (k n) -> p k n", k=KD)
                for k in ks:
                    ins = mm(ps[:, c % 4, 0:T], w[:, k, P * (c % 2):P * (c % 2) + P], mixT[:, k, :],
                             start=k == 0, stop=k == KD - 1)
                    if (c, k) == (2, 6):
                        ins.then_inc(wide_free, 1)
                    elif c >= 4 and c % 2 == 0 and k == 0:
                        ins.then_inc(narrow_free, 1)
                return ins

            W(pool_mixed, 2)
            W(st_copied)
            for c in range(4):
                if c % 2 == 0:
                    pe.wait_ge(*(wide_at(layer, WIDE_OUT) if c == 0 else narrow_at(layer, 0)))
                out_part(c, range(2))
            W(attn_mixed)
            out_part(0, range(2, 6))
            W(gelu_ready)
            W(ada_late, WIDE_ADA - ADA_FIRST)
            for c in range(2):
                for k in range(2):
                    ins = mm(ps[:, 6 + c, 0:T], gluw[:, k, P * c:P * c + P], zv[:, k, :], start=k == 0, stop=k == 1)
            ins.then_inc(glu_made.sem, 1)
            for c in range(1, 4):
                out_part(c, range(2, 6))
            W(ssm_mixed)
            for c in range(4):
                out_part(c, range(6, KD)).then_inc(out_made.sem, 1)
            for c in range(4, KD):
                if c % 2 == 0:
                    pe.wait_ge(*narrow_at(layer, c // 2 - 1))
                W(out_added, c - 3)
                out_part(c, range(KD)).then_inc(out_made.sem, 1)

            W(squares, 2)
            sum_squares(4, sumsq.sem)
            for k in range(KD):
                if k % (KD // 2) == 0:
                    W(h_ready, 3 + k // (KD // 2))
                ins = mm(ps[0:NE, 5, 0:T], rw[:, k, :], hT[:, k, :], start=k == 0, stop=k == KD - 1)
                if k == 0:
                    ins.then_inc(narrow_free, 1)
            ins.then_inc(logits.sem, 1)
            pe.wait_ge(scores_sig.sem, scores_sig.by(layer, 1))
            for t in range(3):
                n = P if t < 2 else NS
                ins = times_one(ps[0:n, 6, NE * t:NE * t + NE], scT[:, P * t:P * t + n], NE)
            ins.then_inc(scores_turned.sem, 1)

            def product(dst, w, w_hi, x, x_hi, first, last_):
                mm(dst, w_hi, x_hi, start=first, stop=False)
                mm(dst, w_hi, x, start=False, stop=False)
                return mm(dst, w, x_hi, start=False, stop=last_)

            def gate_up(e0, j, frees):
                slot = j % 2
                for f in range(4):
                    if f % 2 == 0:
                        W(low_wide, 2 * (e0 + j + 1) + f // 2 + 1)
                    w, w_hi = (t.rearrange("p (k n) -> p k n", k=KD) for t in (r_wide[:, slot, f // 2], r_wide_hi[slot][f // 2]))
                    cols = slice(P * (f % 2), P * (f % 2) + P)
                    for k in range(KD):
                        ins = product(ps[:, f, 0:T], w[:, k, cols], w_hi[:, k, cols], r_h[:, k, :], r_h_hi[:, k, :],
                                      k == 0, k == KD - 1)
                        if frees and f + k == 0:
                            ins.then_inc(frees, 1)
                    if f == 1:
                        ins.then_inc(gate_made.sem, 1)
                return ins

            def down(e0, j, frees):
                slot = j % 2
                W(act_ready, e0 + j + 2)
                W(low_narrow, e0 + j + 2)
                w, w_hi = (t.rearrange("p (k n) -> p k n", k=2) for t in (r_narrow[:, slot], r_narrow_hi[slot]))
                for c in range(KD):
                    pe.wait_ge(down_added.sem, down_added.by(layer, KD * (e0 + j + 1) + max(c + 1, 3)))
                    for k in range(2):
                        cols = slice(P * c, P * c + P)
                        ins = product(ps[:, 5 + c % 3, 0:T], w[:, k, cols], w_hi[:, k, cols], r_act[:, slot, k, :],
                                      r_act_hi[:, slot, k, :], k == 0, k == 1)
                        if frees and c + k == 0:
                            ins.then_inc(frees, 1)
                    ins.then_inc(down_made.sem, 1)

            def spread(e0, j):
                W(ge_ready, e0 + j + 1)
                mm(ps[:, 4, 0:T], r_pick[:, j, :], r_gT[:, 0, :], start=True, stop=False)
                mm(ps[:, 4, 0:T], r_pick[:, j, :], r_gT[:, 1, :], start=False, stop=True).then_inc(gu_made.sem, 1)

            W(out_added, KD)
            W(low_h)
            gate_up(0, -1, None).then_inc(gu_made.sem, 1)
            W(act_step, 2)
            gate_up(0, 0, wide_free)
            W(gates_ready)
            for t in range(3):
                n = P if t < 2 else NS
                ins = times_one(ps[0:NE, 7, P * t:P * t + n], scr[0:n, t, :], n)
            ins.then_inc(gates_turned.sem, 1)
            spread(0, 0)
            down(0, -1, wide_free)

            def step(e0, j):
                W(act_step, 3 * (e0 + j) + 2)
                gate_up(e0, j, narrow_free)
                spread(e0, j)
                down(e0, j - 1, wide_free)

            step(0, 1)
            with pe.Fori(2, NE, 2) as e0:
                for j in range(2):
                    step(e0, j)
            down(NE, -1, narrow_free)
            pe.wait_ge(down_made.sem, down_made.by(layer, KD * (NE + 1)))
            pe.sem_inc(narrow_free, 1)

        pe.wait_ge(last["squares"], 1)
        sum_squares(0, last["sumsq"])
        pe.wait_ge(last["h"], 2)
        for t in range(3):
            n = P if t < 2 else NS
            for g in range(2):
                for k in range(4):
                    ins = turn(ps[0:n, 1 + 2 * t + g, P * k:P * k + P], hT[:, 4 * g + k, P * t:P * t + n], P)
            ins.then_inc(last["turned"], 1)

    @block.scalar
    def _(se):
        act_ = nc.scalar.activation
        chain = Links(se, alink, SCALAR_LINKS)
        se.wait_ge(start_loaded, 16 * 8)
        act_(xrows[0:NC, 3, :], xrows[0:NC, 3, :], ACT.Silu).then_inc(start_silu, 1)
        for h in range(HEADS):
            se.wait_ge(start_ready, KD + h + 1)
            act_(skews[:, h, 0:PAST + 1], ps[:, 4 + h, 0:PAST + 1], ACT.Copy).then_inc(start_copied_a, 1)
        se.wait_ge(skew_moved, 16)
        se.wait_ge(start_vector, 2)
        quarter = sm[:, 0:1]
        with se.Fori(0, DEPTH) as layer:
            chain.enter(layer)

            def W(s, k=1):
                se.wait_ge(s.sem, s.by(layer, k))

            def ada_copy(q, bank):
                W(ada_made, q + 1)
                if q >= 2:
                    W(ada_turned, q - 1)
                dst = (modrow if q < ADA_FIRST else modrow_late)[:, q % 2, :]
                act_(dst, ps[0:NC, bank, :], ACT.Copy).then_inc(ada_copied.sem, 1)

            def ada_columns(q, bank, first):
                W(ada_turned, q + 1)
                act_(modT[:, 4 * q:4 * q + 4, :], ps[:, bank, first:first + 4 * NC].rearrange("p (a b) -> p a b", b=NC),
                     ACT.Copy).then_inc(ada_late.sem, 1)

            W(x_ready)
            act_(hT[:, :, :], xT[:, :, :], ACT.Square).then_inc(squares.sem, 1)
            ada_copy(0, 0)
            ada_copy(1, 1)
            W(rows_copied)
            for h in range(2):
                rows_ = slice(SN * h, SN * h + SN)
                ins = act_(sp_[rows_, 0, :], dtall[rows_, :].rearrange("p (k g) -> p g k", g=2)[:, h, :], ACT.Exp)
            ins.then_inc(dt_ready.sem, 1)
            W(mag_in)
            act_(sp_[:, 2, :], sp_[:, 1, :], ACT.Exp).then_inc(mag_ready.sem, 1)
            W(lam_sums)
            act_(sm[:, 4:6], sm[:, 2:4], ACT.Exp).then_inc(lam_exp.sem, 1)
            ada_copy(2, 0)
            W(angle_ready, 1)
            act_(sp_[:, 7, :], sp_[:, 4, :], ACT.Sin)
            chain(act_(sp_[:, 11, :], sp_[:, 4, :], ACT.Abs))
            act_(sp_[:, 8, :], sp_[:, 11, :], ACT.Sin, bias=quarter, scale=-1.0).then_inc(sines_ready.sem, 1)
            ada_copy(3, 1)
            W(var_ready, 1)
            act_(rstd[:, :], rstd[:, :], ACT.Sqrt).then_inc(sd_ready.sem, 1)
            for c in range(0, PROJ, 2):
                W(proj_made, c + 1)
                act_(projT[:, c, :], ps[:, c % 4, 0:T], ACT.Copy).then_inc(proj_copied_a.sem, 1)
                if c % 4 == 2:
                    p = c // 4
                    W(angle_ready, 2 + p)
                    a0, a1 = ang[:, 2 * (p % 2)], ang[:, 2 * (p % 2) + 1]
                    act_(sinT[:, 2 * p:2 * p + 2, :], a0, ACT.Sin)
                    chain(act_(a1, a0, ACT.Abs))
                    act_(cosT[:, 2 * p:2 * p + 2, :], a1, ACT.Sin, bias=quarter, scale=-1.0).then_inc(sines_ready.sem, 1)
            W(b_turned)
            act_(bbT[:, :, :, :].rearrange("p a b c -> p (a b c)"), ps[:, 7, :], ACT.Copy).then_inc(cb_copied.sem, 1)
            se.wait_ge(cache_stored, layer + 1)
            W(srows_made)
            for n in range(4):
                m = 512 if n < 3 else 256
                ins = act_(rowsS[:, 512 * n:512 * n + m], ps[0:NS, 4 + n, 0:m], ACT.Copy)
            ins.then_inc(srows_copied.sem, 1)
            W(prows_made)
            for n in range(4):
                act_(rowsP[:, n, :], ps[:, n, :], ACT.Copy)
            act_(poolrow[:, :], ps[0:PREV, 7, 256:512], ACT.Copy).then_inc(prows_copied.sem, 1)
            W(dec_max)
            act_(pe64[:, :], pe64[:, :], ACT.Exp, bias=sm[0:ROWS, 9:10], accum_out=sm[0:ROWS, 10:11])\
                .then_inc(dec_exp.sem, 1)
            ada_copy(ADA_FIRST, 0)
            ada_copy(ADA_FIRST + 1, 1)
            ada_columns(ADA_FIRST, 2, 0)
            ada_columns(ADA_FIRST + 1, 3, 0)
            W(dec_pv, NS)
            act_(od, ps[0:32, 5, :], ACT.Copy).then_inc(dec_o_copied.sem, 1)
            W(dec_o_turned)
            def exps(n):
                keys = P * (n % 2 + 1)
                W(negmax, n + 1)
                for m in range(2):
                    ins = act_(sbuf_p[:, n % 2, m, 0:keys], sbuf_s[:, n % 2, m, 0:keys], ACT.Exp,
                               bias=sm[:, 12 + 2 * (n % 2) + m:13 + 2 * (n % 2) + m],
                               accum_out=sm[:, 16 + 2 * (n % 2) + m:17 + 2 * (n % 2) + m])
                ins.then_inc(probs.sem, 1)

            def turned(n):
                h, i = n // 2, n % 2
                W(w_turned, n + 1)
                if h >= 2:
                    W(pv_made, h - 1)
                act_(sbuf_wT[:, h % 2, 0:i + 1, P * i:P * i + P],
                     ps[:, 6 + n % 2, 0:P * (i + 1)].rearrange("p (t q) -> p t q", t=i + 1), ACT.Copy)\
                    .then_inc(w_copied.sem, 1)

            exps(0)
            for n in range(2 * HEADS):
                if n + 1 < 2 * HEADS:
                    exps(n + 1)
                turned(n)
                h = n // 2
                if n % 2 == 0 and h >= 1:
                    ada_columns(ADA_FIRST + 1 + h, 4, 256)
                if n % 2 == 1:
                    ada_copy(ADA_FIRST + 2 + h, 5)
                    W(pv_made, h + 1)
                    act_(oT[:, h, 0:NP_], ps[:, 4, 0:NP_], ACT.Copy).then_inc(pv_copied.sem, 1)
            ada_columns(ADA_FIRST + 1 + HEADS, 4, 256)
            W(o_ready)
            W(pv_copied, HEADS)
            act_(osq, oT[:, :, :], ACT.Square).then_inc(o_squared.sem, 1)
            W(o_var)
            act_(osd, osd, ACT.Sqrt).then_inc(o_sd.sem, 1)
            for c in range(2):
                W(pool_made, c + 1)
                act_(mixT[:, c, :], ps[:, 6 + c, 0:T], ACT.Copy, scale=pT[:, R_PS + c:R_PS + c + 1]).then_inc(pool_mixed.sem, 1)
            for n in range(2):
                ada_copy(WIDE_ADA - 2 + n, 6 + n)
                ada_columns(WIDE_ADA - 2 + n, 6 + n, 0)
            W(st_turned)
            act_(strow[0:2 * SC, 0, :], ps[0:2 * SC, 0, 0:P], ACT.Copy)
            act_(strow[:, 1, :], ps[:, 1, 0:P], ACT.Copy).then_inc(st_copied.sem, 1)
            W(o_normed)
            act_(mixT[:, 2:6, :], osd, ACT.Copy, scale=sm[:, 7:8]).then_inc(attn_mixed.sem, 1)
            W(y_ready)
            act_(zv, yv, ACT.Gelu_apprx_tanh).then_inc(gelu_ready.sem, 1)
            W(glu_made)
            for c in range(2):
                ins = act_(gv[:, c, :], ps[:, 6 + c, 0:T], ACT.Sigmoid, bias=pT[:, R_GB + c:R_GB + c + 1])
            ins.then_inc(glu_gate.sem, 1)
            W(out_added, KD)
            W(pool_prompt)
            act_(hT[:, :, :], xT[:, :, :], ACT.Square).then_inc(squares.sem, 1)
            W(ssm_mixed)

            def high_wide_part(slot, at):
                se.wait_ge(*at)
                for t in range(2):
                    act_(r_wide_hi[slot][t], wide[:, slot, t], ACT.Copy).then_inc(high_wide.sem, 1)

            def high_narrow_part(slot, at):
                se.wait_ge(*at)
                act_(r_narrow_hi[slot], narrow[:, slot], ACT.Copy).then_inc(high_narrow.sem, 1)

            high_wide_part(1, unit_wide(layer, 0, -1))
            W(var_ready, 2)
            act_(rstd[:, :], rstd[:, :], ACT.Sqrt).then_inc(sd_ready.sem, 1)
            W(h_ready, 4)
            act_(r_h_hi[:, :, :], hT[:, :, :], ACT.Copy).then_inc(high_h.sem, 1)
            W(logits)
            act_(scT, ps[0:NE, 5, 0:T], ACT.Sigmoid).then_inc(scores_sig.sem, 1)
            high_wide_part(0, unit_wide(layer, 0, 0))
            high_narrow_part(1, unit_narrow(layer, 0, -1))

            def silu_gate(e0, j):
                W(gate_made, e0 + j + 2)
                act_(silu[:, j % 2], ps[:, 0:2, 0:T], ACT.Silu).then_inc(silu_ready.sem, 1)

            silu_gate(0, -1)
            high_wide_part(1, unit_wide(layer, 0, 1))
            se.wait_ge(cache_stored, layer + 2)
            high_narrow_part(0, unit_narrow(layer, 0, 0))
            silu_gate(0, 0)
            high_wide_part(0, unit_wide(layer, 0, 2))
            high_narrow_part(1, unit_narrow(layer, 0, 1))
            silu_gate(0, 1)
            high_wide_part(1, unit_wide(layer, 0, 3))
            high_narrow_part(0, unit_narrow(layer, 0, 2))
            with se.Fori(2, NE - 2, 2) as e0:
                for j in range(2):
                    silu_gate(e0, j)
                    high_wide_part(j, unit_wide(layer, e0, j + 2))
                    high_narrow_part(1 - j, unit_narrow(layer, e0, j + 1))
            silu_gate(NE - 2, 0)
            high_narrow_part(1, unit_narrow(layer, NE - 2, 1))
            silu_gate(NE - 2, 1)
            chain.check()
        se.wait_ge(x_ready.sem, DEPTH + 1)
        act_(hT[:, :, :], xT[:, :, :], ACT.Square).then_inc(last["squares"], 1)
        se.wait_ge(last["var"], 1)
        act_(rstd[:, :], rstd[:, :], ACT.Sqrt).then_inc(last["sd"], 1)
        yrows = projT[:, :, :].rearrange("p a b -> p (a b)")[:, 0:3 * D].rearrange("p (a b) -> p a b", a=3)
        for t in range(3):
            n = P if t < 2 else NS
            se.wait_ge(last["turned"], t + 1)
            for g in range(2):
                act_(yrows[0:n, t, 512 * g:512 * g + 512], ps[0:n, 1 + 2 * t + g, :], ACT.Copy).then_inc(last["copied"], 1)

    @block.vector
    def _(dve):
        v = nc.vector
        ts, tt, stt, cp = v.tensor_scalar, v.tensor_tensor, v.scalar_tensor_tensor, v.tensor_copy
        chain = Links(dve, vlink, VECTOR_LINKS)
        v.memset(sm[:, 0:1], math.pi / 2)
        dve.wait_ge(start_loaded, 16 * 8)
        cp(relbw[:, :, :], relb[:, :].unsqueeze(2).to_broadcast([32, HEADS, P]))
        for m in range(2):
            ins = cp(relbs[:, :, :, m], relb[:, :].unsqueeze(1).to_broadcast([32, NS, HEADS]))
        ins.then_inc(start_vector, 1)
        for k in range(KD):
            dve.wait_ge(start_ready, k + 1)
            cp(xT[:, k, :], ps[:, k % 4, 0:T]).then_inc(start_copied_v, 1)
        dve.wait_ge(start_ready, KD + HEADS + 1)
        dve.wait_ge(start_copied_a, HEADS)
        cp(condT[:, :, :].rearrange("p a b -> p (a b)"), ps[:, 0, 0:KD * NC])
        cp(finalg[:, :], ps[:, 1, 0:KD])
        chain(cp(biasS[:, :], ps[0:ROWS, 2, 0:PAST + 1]))
        dve.sem_inc(params_free, 1)
        dve.sem_inc(x_ready.sem, 1)
        dve.sem_inc(down_added.sem, 3)
        dve.sem_inc(start_vector, 1)
        dve.wait_ge(skew_moved, 16 * (1 + HEADS))

        def held():
            ticks[1] += 1
            v.memset(tick_v[:, ticks[1] - 1:ticks[1]], 0.0)

        def norm(wait_sum, bank, var_done, wait_sd, A, B, done):
            wait_sum()
            ts(rstd[:, :], ps[:, bank, 0:T], 1.0 / D, EPS, ALU.mult, ALU.add).then_inc(var_done, 1)
            wait_sd()
            chain(v.reciprocal(rstd[:, :], rstd[:, :]))
            halves = [slice(0, KD // 2), slice(KD // 2, KD)]
            scaled = [chain.mark(tt(hT[:, ks, :], xT[:, ks, :], rstd[:, :].unsqueeze(1).to_broadcast([P, KD // 2, T]), ALU.mult))
                      for ks in halves]
            for ks, link in zip(halves, scaled):
                chain.wait(link)
                if B is None:
                    for k in range(ks.start, ks.stop):
                        ins = ts(hT[:, k, :], hT[:, k, :], A[:, k:k + 1], None, ALU.mult)
                else:
                    decode = chain.mark(tt(hT[:, ks, NP_:T], hT[:, ks, NP_:T], A[:, ks, 1:NC], ALU.mult))
                    for k in range(ks.start, ks.stop):
                        ts(hT[:, k, 0:NP_], hT[:, k, 0:NP_], A[:, k, 0:1], B[:, k, 0:1], ALU.mult, ALU.add)
                    chain.wait(decode)
                    ins = tt(hT[:, ks, NP_:T], hT[:, ks, NP_:T], B[:, ks, 1:NC], ALU.add)
                ins.then_inc(done, 1)

        with dve.Fori(0, DEPTH) as layer:
            chain.enter(layer)

            def W(s, k=1):
                dve.wait_ge(s.sem, s.by(layer, k))

            S = lambda n: sp_[:, n, :]
            W(params_loaded, 16 * N_PARAM)
            cp(selb[:, :, :], cst[0:NS, K_ID:K_ID + NS].unsqueeze(2).to_broadcast([NS, NS, P]))
            for d in range(2):
                ins = cp(crow2[:, :, :, SN * d:SN * d + SN], crow[:, :, :, :])
            ins.then_inc(crow_ready.sem, 1)
            for n in range(2):
                chain(tt(lamv[:, 2 * n, :], lamv[:, 2 * n, :], lamv[:, 2 * n + 1, :], ALU.mult))
                ins = v.tensor_reduce(sm[:, 2 + n:3 + n], lamv[:, 2 * n, :], AX.X, ALU.add)
            ins.then_inc(lam_sums.sem, 1)
            W(rows_turned)
            cp(h0T[:, :, :, :].rearrange("p a b c -> p (a b c)"), ps[:, 4, P:2 * P])
            for c in range(2):
                cp(ueS[:, c, :, 0:PREV], ps[:, 5, P * c:P * c + NS * PREV].rearrange("p (b t) -> p b t", b=NS))
            cp(pT[:, :], ps[:, 4, 0:R_ALL]).then_inc(rows_copied.sem, 1)
            W(rows_copied)
            W(dt_ready)
            tt(S(3), pT[:, R_AI:R_AI + SC], S(0), ALU.mult)
            tt(S(1), pT[:, R_AR:R_AR + SC], S(0), ALU.mult).then_inc(mag_in.sem, 1)
            W(mag_in)
            chain(ts(S(6), S(3), 1.0 / (2 * math.pi), ROUND, ALU.mult, ALU.add))
            chain(ts(S(6), S(6), ROUND, None, ALU.subtract))
            chain(stt(S(4), S(6), -TWO_PI_A, S(3), ALU.mult, ALU.add))
            chain(stt(S(4), S(6), -TWO_PI_B, S(4), ALU.mult, ALU.add))
            ts(S(4), S(4), -3.1415925, 3.1415925, ALU.max, ALU.min).then_inc(angle_ready.sem, 1)
            W(angle_ready, 1)
            ts(S(5), S(4), 1.0 / (2 * math.pi), None, ALU.mult)
            chain(ts(S(12), S(4), ROUND / 1024, ROUND / 1024, ALU.add, ALU.subtract))
            chain(tt(S(13), S(4), S(12), ALU.subtract))
            tcol = cst[:, K_T:K_T + NP_]

            def angles(p):
                if p >= 2:
                    W(sines_ready, p)
                a0, a1 = ang[:, 2 * (p % 2)], ang[:, 2 * (p % 2) + 1]
                for j in range(2):
                    c = 2 * p + j
                    ts(a0[:, j, :], tcol, sp_[:, 12, c:c + 1], None, ALU.mult)
                    ins = ts(a1[:, j, :], tcol, sp_[:, 5, c:c + 1], ROUND, ALU.mult, ALU.add)
                chain(ins)
                chain(ts(a1, a1, ROUND, None, ALU.subtract))
                chain(stt(a0, a1, -TWO_PI_A, a0, ALU.mult, ALU.add))
                chain(stt(a0, a1, -TWO_PI_B, a0, ALU.mult, ALU.add))
                for j in range(2):
                    c = 2 * p + j
                    ins = stt(a0[:, j, :], tcol, sp_[:, 13, c:c + 1], a0[:, j, :], ALU.mult, ALU.add)
                chain(ins)
                ts(a0, a0, -3.1415925, 3.1415925, ALU.max, ALU.min).then_inc(angle_ready.sem, 1)
                if p == 0:
                    W(sines_ready, 1)
                    W(mag_ready)
                    tt(S(9), S(2), S(8), ALU.mult)
                    tt(S(10), S(2), S(7), ALU.mult)
                    tt(S(14), pT[:, R_AR:R_AR + SC], pT[:, R_AR:R_AR + SC], ALU.mult)
                    chain(tt(S(15), pT[:, R_AI:R_AI + SC], pT[:, R_AI:R_AI + SC], ALU.mult))
                    tt(S(14), S(14), S(15), ALU.add)
                    chain(ts(S(16), S(9), 1.0, None, ALU.subtract))
                    v.reciprocal(S(14), S(14))
                    tt(S(17), S(16), pT[:, R_AR:R_AR + SC], ALU.mult)
                    tt(S(18), S(10), pT[:, R_AI:R_AI + SC], ALU.mult)
                    tt(S(19), S(10), pT[:, R_AR:R_AR + SC], ALU.mult)
                    chain(tt(S(20), S(16), pT[:, R_AI:R_AI + SC], ALU.mult))
                    tt(S(17), S(17), S(18), ALU.add)
                    chain(tt(S(19), S(19), S(20), ALU.subtract))
                    tt(S(17), S(17), S(14), ALU.mult)
                    chain(tt(S(19), S(19), S(14), ALU.mult))
                    wide_ = lambda s: s.unsqueeze(2).to_broadcast([P, SC, SCH])
                    tt(bpad[:, 0, :, 0, :], bst[:, 0], wide_(S(17)), ALU.mult)
                    tt(bpad[:, 0, :, 1, :], bst[:, 1], wide_(S(19)), ALU.mult)
                    tt(bpad[:, 1, :, 0, :], bst[:, 1], wide_(S(17)), ALU.mult)
                    chain(tt(bpad[:, 1, :, 1, :], bst[:, 0], wide_(S(19)), ALU.mult))
                    tt(bb[:, 0], bpad[:, 0, :, 0, :], bpad[:, 0, :, 1, :], ALU.subtract)
                    chain(tt(bb[:, 1], bpad[:, 1, :, 0, :], bpad[:, 1, :, 1, :], ALU.add))
                    for r in range(2):
                        for h in range(2):
                            ins = ts(bpad[:, r, :, h, :], bb[:, r], half[:, h:h + 1], None, ALU.mult)
                    ins.then_inc(bpad_ready.sem, 1)
                    wide_ = lambda s: s.unsqueeze(2).to_broadcast([P, SC, NS])
                    h0 = [h0T[:, r].rearrange("p b k -> p k b") for r in range(2)]
                    tt(i0[:, 0], h0[0], wide_(S(9)), ALU.mult)
                    tt(i0t[:, 0], h0[1], wide_(S(10)), ALU.mult)
                    tt(i0[:, 1], h0[1], wide_(S(9)), ALU.mult)
                    chain(tt(i0t[:, 1], h0[0], wide_(S(10)), ALU.mult))
                    tt(i0[:, 0], i0[:, 0], i0t[:, 0], ALU.subtract)
                    tt(i0[:, 1], i0[:, 1], i0t[:, 1], ALU.add)
                    W(lam_exp)
                    chain(tt(sm[:, 6:7], sm[:, 5:6], sm[:, 4:5], ALU.subtract))
                    tt(sm[:, 6:7], sm[:, 6:7], cst[:, bass.ds(K_LAM + 2 * layer, 1)], ALU.subtract)
                    chain(tt(sm[:, 7:8], pT[:, R_SUB:R_SUB + 1], cst[:, bass.ds(K_LAM + 1 + 2 * layer, 1)], ALU.mult))

            W(ada_turned, ADA_FIRST)
            tt(modT[:, 0:16, :], ps[:, 2, 0:16 * NC].rearrange("p (a b) -> p a b", b=NC),
               pT[:, R_BADA:R_BADA + 16].unsqueeze(2).to_broadcast([P, 16, NC]), ALU.add).then_inc(mod_ready.sem, 1)
            W(mod_ready, 1)

            def scale_of_norm(n, c, r):
                chain(ts(scA[:, n], modT[:, c:c + 8, :], 1.0, None, ALU.add))
                chain(tt(scA[:, n], scA[:, n], pT[:, r:r + 8].unsqueeze(2).to_broadcast([P, KD, NC]), ALU.mult))

            scale_of_norm(0, 8, R_N1)
            norm(lambda: W(sumsq, 1), 3, var_ready.sem, lambda: W(sd_ready, 1), scA[:, 0], modT[:, 0:8, :], h_ready.sem)
            neglam = sm[:, 6:7]
            for c in range(1, PROJ, 2):
                W(proj_made, c + 1)
                cp(projT[:, c, :], ps[:, c % 4, 0:T]).then_inc(proj_copied_v.sem, 1)
                if c % 4 == 1:
                    angles(c // 4)
            W(c_turned)
            for r in range(2):
                for h in range(2):
                    src = ps[:, 6, 256 * r:256 * r + 256].rearrange("p (t k h c) -> p t k h c", t=2, k=4, h=2)[:, :, :, h, :]
                    dst = cT[:, r].rearrange("p t (k h c) -> p t k h c", k=4, h=2)[:, :, :, h, :]
                    for t in range(2):
                        ins = ts(dst[:, t], src[:, t], half[:, h:h + 1], -1.0 if r else 1.0, ALU.mult, ALU.mult)
            ins.then_inc(cb_copied.sem, 1)
            W(proj_copied_v, PROJ // 2)
            W(proj_copied_a, PROJ // 2)
            W(sines_ready, 1 + SC // 2)
            for c in range(2):
                ins = cp(ueS[:, c, :, PREV], projT[:, c, NP_:T])
            chain(ins)
            for n, w in enumerate(WINDOWS):
                rows_, c = slice(64 * (n % 2), 64 * (n % 2) + 64), n // 2
                ins = v.tensor_reduce(pooled[rows_, c, NP_:T], ueS[rows_, c, :, PREV + 1 - w:], AX.X, ALU.add)
            chain(ins)
            for n, w in enumerate(WINDOWS):
                rows_, c = slice(64 * (n % 2), 64 * (n % 2) + 64), n // 2
                ins = ts(pooled[rows_, c, NP_:T], pooled[rows_, c, NP_:T], 1.0 / w, None, ALU.mult)
            chain(ins)
            tt(pooled[:, :, NP_:T], pooled[:, :, NP_:T], projT[:, 0:2, NP_:T], ALU.subtract).then_inc(pool_sample.sem, 1)

            qs = projT[:, C_Q:C_Q + HEADS, NP_:T].rearrange("p h b -> p b h")
            ks = projT[:, C_K:C_K + HEADS, NP_:T].rearrange("p h b -> p b h")
            chain(tt(qk[:, :, :], qs, ks, ALU.mult))
            for m in range(2):
                ts(prodm[:, :, :, m], qk[:, :, :], half[:, m:m + 1], None, ALU.mult)
            for b in range(NS):
                W(q_spread, b + 1)
                dve.wait_ge(k_loaded[b % 2].sem, k_loaded[b % 2].by(layer, 32 * (b // 2 + 1)))
                for g in range(PAGES):
                    ins = tt(prod[:, g, :], ps[:, 4 + b % 2, :], kbuf[:, b % 2, g, :], ALU.mult)
                ins.then_inc(dec_products.sem, 1)
                W(dec_products, b + 1)
                ins = v.tensor_reduce(decS[:, :, 8 * b:8 * b + 8], prod.rearrange("p g (a d) -> p g a d", d=HD), AX.X, ALU.add)
                if b == NS - 1:
                    ins.then_inc(dec_scored.sem, 1)
                else:
                    chain(ins)
            W(dec_turned)
            chain(stt(pe64[:, :], ps[0:ROWS, 6, 0:PAST + 1], HD ** -0.5, biasS[:, :], ALU.mult, ALU.add))
            chain(v.reduce_max(sm[0:ROWS, 8:9], pe64[:, :], AX.X))
            ts(sm[0:ROWS, 9:10], sm[0:ROWS, 8:9], -1.0, None, ALU.mult).then_inc(dec_max.sem, 1)
            W(dec_exp)
            v.reciprocal(sm[0:ROWS, 11:12], sm[0:ROWS, 10:11])
            chain(stt(sm[0:ROWS, 8:9], cst[0:ROWS, K_M1:K_M1 + 1], sm[0:ROWS, 6:7], cst[0:ROWS, K_M0:K_M0 + 1], ALU.mult, ALU.add))
            ts(aps[:, :], cst[0:ROWS, K_AB:K_AB + NS], pe64[:, PAST:PAST + 1], None, ALU.mult)
            ts(comb[:, :], cst[0:ROWS, K_CMB:K_CMB + 32], sm[0:ROWS, 8:9], sm[0:ROWS, 11:12], ALU.mult, ALU.mult)\
                .then_inc(comb_ready.sem, 1)
            W(dec_weights)
            cp(wself[:, :], ps[0:NS, 7, 64:96])
            for g in range(PAGES):
                for b in range(NS):
                    ins = cp(w32[:, g, b, 4 * b:4 * b + 4], ps[:, 7, 32 * g + 4 * b:32 * g + 4 * b + 4])
            ins.then_inc(w32_ready.sem, 1)

            def biased_scores(n):
                h, i = n // 2, n % 2
                keys = P * (i + 1)
                W(scored, n + 1)
                if n >= 2:
                    W(probs, n - 1)
                s = sbuf_s[:, n % 2, :, 0:keys]
                stt(s, ps[:, 2 * (n % 2):2 * (n % 2) + 2, 0:keys], HD ** -0.5,
                    biasT[:, h, NP_ - keys:NP_].unsqueeze(1).to_broadcast([P, 2, keys]), ALU.mult, ALU.add)\
                    .then_inc(biased_ready.sem, 1)
                W(biased_ready, n + 1)
                mx = sm[:, 20 + 2 * (n % 2):22 + 2 * (n % 2)]
                chain(v.tensor_reduce(mx, s, AX.X, ALU.max))
                ts(sm[:, 12 + 2 * (n % 2):14 + 2 * (n % 2)], mx, -1.0, None, ALU.mult).then_inc(negmax.sem, 1)

            def weights(n):
                keys = P * (n % 2 + 1)
                W(probs, n + 1)
                if n >= 2:
                    W(w_turned, n - 1)
                p_ = sbuf_p[:, n % 2]
                rs = sm[:, 24:26]
                chain(v.reciprocal(rs, sm[:, 16 + 2 * (n % 2):18 + 2 * (n % 2)]))
                tt(sm[:, 26:27], rs[:, 1:2], neglam, ALU.mult)
                chain(ts(sbuf_w0[:, 0:keys], p_[:, 0, 0:keys], rs[:, 0:1], None, ALU.mult))
                stt(sbuf_w[:, n % 2, 0:keys], p_[:, 1, 0:keys], sm[:, 26:27], sbuf_w0[:, 0:keys], ALU.mult, ALU.add)\
                    .then_inc(w_ready.sem, 1)

            W(dec_o_turned)
            for h in range(HEADS):
                ins = cp(oT[:, h, NP_:T], ps[:, 5, 32 * h:32 * h + 32].rearrange("p (b h) -> p h b", h=HEADS)[:, h, :])
            ins.then_inc(o_ready.sem, 1)
            biased_scores(0)
            for n in range(2 * HEADS):
                if n + 1 < 2 * HEADS:
                    biased_scores(n + 1)
                weights(n)
            W(w_ready, 2 * HEADS)

            for p in range(SC // 2):
                W(bu_made, p + 1)
                C, Sn = cosT[:, 2 * p:2 * p + 2, :], sinT[:, 2 * p:2 * p + 2, :]
                br, bi = ps[:, 0:2, 0:NP_], ps[:, 2:4, 0:NP_]
                R = lambda n: rot[:, n]
                tt(R(0), C, br, ALU.mult)
                tt(R(1), Sn, bi, ALU.mult)
                tt(R(2), C, bi, ALU.mult)
                chain(tt(R(3), Sn, br, ALU.mult))
                tt(R(0), R(0), R(1), ALU.add)
                chain(tt(R(2), R(2), R(3), ALU.subtract))
                for j in range(2):
                    mag = sp_[:, 2, 2 * p + j:2 * p + j + 1].to_broadcast([P, NP_])
                    v.tensor_tensor_scan(R(4)[:, j, :], mag, R(0)[:, j, :], 0.0, ALU.mult, ALU.add)
                    ins = v.tensor_tensor_scan(R(5)[:, j, :], mag, R(2)[:, j, :], 0.0, ALU.mult, ALU.add)
                chain(ins)
                if p >= 1:
                    W(y_made, p)
                for r in range(2):
                    ins = tt(hs[:, r, :, NP_:T], ps[:, 2 * r:2 * r + 2, NP_:T], i0[:, r, 2 * p:2 * p + 2, :], ALU.add)
                ins.then_inc(bu_used.sem, 1)
                tt(R(0), C, R(4), ALU.mult)
                tt(R(1), Sn, R(5), ALU.mult)
                tt(R(2), Sn, R(4), ALU.mult)
                chain(tt(R(3), C, R(5), ALU.mult))
                tt(hs[:, 0, :, 0:NP_], R(0), R(1), ALU.subtract)
                tt(hs[:, 1, :, 0:NP_], R(2), R(3), ALU.add).then_inc(hs_ready.sem, 1)
                W(hs_ready, p + 1)
                for r in range(2):
                    cp(stF[:, r, 2 * p:2 * p + 2], hs[:, r, :, NP_ - 1])
                    ins = cp(stS[:, r, :, 2 * p:2 * p + 2], hs[:, r, :, NP_:T].rearrange("p k b -> p b k"))
                if p == 0:
                    W(o_sums)
                    ts(osd, ps[:, 4:4 + HEADS, 0:T], 1.0 / VD, EPS, ALU.mult, ALU.add).then_inc(o_var.sem, 1)
                if p == SC // 2 - 1:
                    ins.then_inc(st_ready.sem, 1)
            W(o_sd)
            W(o_ready)
            W(pv_copied, HEADS)
            chain(v.reciprocal(osd, osd))
            tt(osd, osd, oT[:, :, :], ALU.mult).then_inc(o_normed.sem, 1)
            W(ada_late, WIDE_ADA - ADA_FIRST)
            tt(modT[:, 16:48, :], modT[:, 16:48, :],
               pT[:, R_BADA + 16:R_BADA + 48].unsqueeze(2).to_broadcast([P, 32, NC]), ALU.add).then_inc(mod_ready.sem, 1)
            W(mod_ready, 2)
            scale_of_norm(1, 32, R_N2)
            W(y_made, SC // 2)
            W(st_ready)
            for c in range(2):
                ins = stt(yv[:, c, :], projT[:, C_U + c, :], pT[:, R_SD + c:R_SD + c + 1], ps[:, 4 + c, 0:T], ALU.mult, ALU.add)
            ins.then_inc(y_ready.sem, 1)
            W(glu_gate)
            tt(mixT[:, 6:8, :], zv, gv, ALU.mult).then_inc(ssm_mixed.sem, 1)

            for c in range(KD):
                W(out_made, c + 1)
                g = modT[:, 16 + c, :]
                tt(sm[:, 32 + 8 * (c % 2):40 + 8 * (c % 2)], ps[:, c % 4, NP_:T], g[:, 1:NC], ALU.mult)
                chain(stt(xT[:, c, 0:NP_], ps[:, c % 4, 0:NP_], g[:, 0:1], xT[:, c, 0:NP_], ALU.mult, ALU.add))
                tt(xT[:, c, NP_:T], xT[:, c, NP_:T], sm[:, 32 + 8 * (c % 2):40 + 8 * (c % 2)], ALU.add).then_inc(out_added.sem, 1)
            W(out_added, KD)
            def low_wide_part(slot, e0, j, parts=range(2)):
                for t in parts:
                    W(high_wide, 2 * (e0 + j + 1) + t + 1)
                    tt(r_wide[:, slot, t], wide[:, slot, t], plain(r_wide_hi[slot][t]), ALU.subtract).then_inc(low_wide.sem, 1)

            def low_narrow_part(slot, e0, j):
                W(high_narrow, e0 + j + 2)
                tt(r_narrow[:, slot], narrow[:, slot], plain(r_narrow_hi[slot]), ALU.subtract).then_inc(low_narrow.sem, 1)

            low_wide_part(1, 0, -1, (0,))
            norm(lambda: W(sumsq, 2), 4, var_ready.sem, lambda: W(sd_ready, 2), scA[:, 1], modT[:, 24:32, :], h_ready.sem)
            W(high_h)
            W(logits)
            tt(r_h[:, :, :], hT[:, :, :], plain(r_h_hi[:, :, :]), ALU.subtract).then_inc(low_h.sem, 1)
            low_wide_part(1, 0, -1, (1,))
            low_wide_part(0, 0, 0)

            def add(e0, j, chunks):
                n = e0 + j + 1
                if chunks[0] == 0:
                    W(down_added, KD * n + 3)
                for c in chunks:
                    W(down_made, KD * n + c + 1)
                    tt(acc[:, c, :], acc[:, c, :], ps[:, 5 + c % 3, 0:T], ALU.add).then_inc(down_added.sem, 1)

            def activate(e0, j):
                slot, steps = j % 2, 3 * (e0 + j + 1)
                shared = isinstance(e0, int) and e0 + j < 0
                W(silu_ready, e0 + j + 2)
                W(gu_made, e0 + j + 2)
                if shared:
                    tt(act[:, slot], silu[:, slot], ps[:, 2:4, 0:T], ALU.mult).then_inc(act_step.sem, 2)
                else:
                    tt(silu[:, slot], silu[:, slot], ps[:, 2:4, 0:T], ALU.mult).then_inc(act_step.sem, 1)
                    add(e0, j - 1, (0, 1))
                    W(act_step, steps + 1)
                    tt(act[:, slot], silu[:, slot], ps[:, 4, 0:T].unsqueeze(1).to_broadcast([P, 2, T]), ALU.mult)\
                        .then_inc(act_step.sem, 1)
                    add(e0, j - 1, (2, 3))
                W(act_step, steps + 2)
                cp(r_act_hi[:, slot], act[:, slot]).then_inc(act_step.sem, 1)
                if not shared:
                    add(e0, j - 1, (4, 5))
                W(act_step, steps + 3)
                tt(r_act[:, slot], act[:, slot], plain(r_act_hi[:, slot]), ALU.subtract).then_inc(act_ready.sem, 1)
                if not shared:
                    add(e0, j - 1, (6, 7))

            W(scores_turned)
            cp(scr[:, 0:2, :], ps[:, 6, 0:2 * NE].rearrange("p (t e) -> p t e", t=2))
            chain(cp(scr[0:NS, 2, :], ps[0:NS, 6, 2 * NE:3 * NE]))
            chain(tt(biased[:, :, :], scr[:, :, :], rbias[:, :].unsqueeze(1).to_broadcast([P, 3, NE]), ALU.add))
            held()
            for t in range(3):
                for g in range(NG):
                    ins = v.max(g8[:, t, g, :], biased[:, t, PG * g:PG * g + PG])
            chain(ins)
            chain(tt(g1[:, :, :], g8[:, :, :, 0], g8[:, :, :, 1], ALU.add))
            low = cst[:, K_LOW:K_LOW + NG * NG].rearrange("p (i j) -> p i j", i=NG)
            for t in range(3):
                me = g1[:, t, :].unsqueeze(2).to_broadcast([P, NG, NG])
                other = g1[:, t, :].unsqueeze(1).to_broadcast([P, NG, NG])
                tt(pairs[:, t], other, me, ALU.is_gt)
                ins = tt(pairs2[:, t], other, me, ALU.is_equal)
            chain(ins)
            for t in range(3):
                ins = tt(pairs2[:, t], pairs2[:, t], low, ALU.mult)
            chain(ins)
            chain(tt(pairs[:, :, :, :], pairs[:, :, :, :], pairs2[:, :, :, :], ALU.add))
            chain(v.tensor_reduce(rank[:, :, :], pairs[:, :, :, :], AX.X, ALU.add))
            activate(0, -1)
            chain(ts(rank[:, :, :], rank[:, :, :], float(TOPG), NEG, ALU.is_ge, ALU.mult))
            chain(tt(masked[:, :, :].rearrange("p t (g e) -> p (t g) e", g=NG), biased[:, :, :].rearrange("p t (g e) -> p (t g) e", g=NG),
                     rank[:, :, :].rearrange("p t g -> p (t g)").unsqueeze(2).to_broadcast([P, 3 * NG, PG]), ALU.add))
            held()
            for t in range(3):
                ins = v.max(t8[:, t, :], masked[:, t, :])
            chain(ins)
            held()
            for t in range(3):
                ins = v.match_replace(masked[:, t, :], t8[:, t, :], masked[:, t, :], 3 * NEG)
            chain(ins)
            chain(ts(masked[:, :, :], masked[:, :, :], 2 * NEG, None, ALU.is_le))
            chain(tt(scr[:, :, :], scr[:, :, :], masked[:, :, :], ALU.mult))
            chain(v.tensor_reduce(gsum[:, :], scr[:, :, :], AX.X, ALU.add))
            chain(ts(gsum[:, :], gsum[:, :], 1e-30, None, ALU.max))
            chain(v.reciprocal(gsum[:, :], gsum[:, :]))
            for t in range(3):
                ins = ts(scr[:, t, :], scr[:, t, :], gsum[:, t:t + 1], SCALE_R, ALU.mult, ALU.mult)
            ins.then_inc(gates_ready.sem, 1)
            dve.sem_inc(params_free, 1)

            def pick_expert(slot, e):
                col = cst[0:NE, K_ID + e:K_ID + e + 1] if isinstance(e, int) else cst[0:NE, bass.ds(K_ID + e, 1)]
                ts(r_pick[:, slot, :], ones[0:NE, :], col, None, ALU.mult).then_inc(ge_ready.sem, 1)

            low_narrow_part(1, 0, -1)
            W(gates_turned)
            chain(cp(r_gT[:, 0, :], ps[0:NE, 7, 0:T]))
            chain(tt(r_gT[:, 1, :], ps[0:NE, 7, 0:T], plain(r_gT[:, 0, :]), ALU.subtract))
            pick_expert(0, 0)
            pick_expert(1, 1)
            dve.wait_ge(acc_zero.sem, acc_zero.by(layer, 1))

            def unit(e0, j, wide_too, narrow_too):
                activate(e0, j)
                pick_expert(j, e0 + j + 2)
                if isinstance(e0, int) and e0 + j == 0:
                    low_wide_part(1, 0, 1)
                    low_narrow_part(0, 0, 0)
                if wide_too:
                    low_wide_part(j, e0, j + 2)
                if narrow_too:
                    low_narrow_part(1 - j, e0, j + 1)

            for j in range(2):
                unit(0, j, True, True)
            with dve.Fori(2, NE - 2, 2) as e0:
                for j in range(2):
                    unit(e0, j, True, True)
            unit(NE - 2, 0, False, True)
            unit(NE - 2, 1, False, False)
            add(NE, -1, range(KD))
            W(down_added, KD * (NE + 1) + 3)
            for c in range(KD):
                stt(xT[:, c, 0:NP_], acc[:, c, 0:NP_], modT[:, 40 + c, 0:1], xT[:, c, 0:NP_], ALU.mult, ALU.add)
            chain(tt(acc[:, :, NP_:T], acc[:, :, NP_:T], modT[:, 40:48, 1:NC], ALU.mult))
            tt(xT[:, :, NP_:T], xT[:, :, NP_:T], acc[:, :, NP_:T], ALU.add).then_inc(x_ready.sem, 1)
            chain.check()
        chain.leave()
        norm(lambda: dve.wait_ge(last["sumsq"], 1), 0, last["var"], lambda: dve.wait_ge(last["sd"], 1),
             finalg, None, last["h"])

    for cm in reversed(ctx_list):
        cm.__exit__(None, None, None)


SCALAR_LINKS, VECTOR_LINKS = 5, 135

OUTPUTS = [
    ("y_prompt", (1, NP_, D)), ("y_sample", (NS, 1, D)),
    ("k_prompt", (1, DEPTH, NP_, HEADS, 2 * HD)), ("v_prompt", (1, DEPTH, NP_, HEADS, VD)),
    ("pool_prompt", (1, DEPTH, PREV, POOL_W)),
    ("ssm_re_prompt", (1, DEPTH, SG, SN)), ("ssm_im_prompt", (1, DEPTH, SG, SN)),
    ("k_sample", (NS, DEPTH, 1, HEADS, 2 * HD)), ("v_sample", (NS, DEPTH, 1, HEADS, VD)),
    ("pool_sample", (NS, DEPTH, PREV, POOL_W)),
    ("ssm_re_sample", (NS, DEPTH, SG, SN)), ("ssm_im_sample", (NS, DEPTH, SG, SN)),
]


def kernel(**inputs):
    import concourse.bacc as bacc
    from concourse.bass_utils import run_bass_kernel_spmd

    nc = bacc.Bacc("TRN2", target_bir_lowering=False, num_devices=1)
    arrays, ins = {}, {}
    for name, x in [*inputs.items(), ("consts", shape_constants())]:
        x = np.ascontiguousarray(x)
        arrays[f"in_{name}"] = x
        ins[name] = nc.dram_tensor(f"in_{name}", x.shape, mybir.dt.from_np(x.dtype), kind="ExternalInput").ap()
    outs = {name: nc.dram_tensor(f"out_{name}", shape, F32, kind="ExternalOutput").ap() for name, shape in OUTPUTS}
    program(nc, ins, outs)
    r = run_bass_kernel_spmd(nc, [arrays], core_ids=[0])
    return tuple(r.results[0][f"out_{name}"] for name, _ in OUTPUTS)
```
